# Optimizing a Trainium2 kernel written in Bass

```python
import math
import jax, jax.numpy as jnp
from jax import lax
import numpy as np

D_MODEL = 2048
BATCH = 1
SEQ = 128
DEPTH = 2
DEC_BATCH = 1
DEC_SEQ = 128
PAST_LEN = 128

GRID_W = 64
N_MIXERS = 2
NA_HEADS = 16
NA_HEAD_DIM = D_MODEL // NA_HEADS
WIN_ROWS_MAX = 8
WIN_COLS = 16
Q_COL_BLOCK = 16
K_COL_BAND = Q_COL_BLOCK + WIN_COLS
CTX_Q_BLOCK = 128
SSM_D_INNER = 2 * D_MODEL
SSM_HEAD_DIM = 64
SSM_HEADS = SSM_D_INNER // SSM_HEAD_DIM
SSM_GROUPS = 8
SSM_STATE = 128
SSM_CONV = 3
SSM_CHUNK = 128
SSM_CONV_DIM = SSM_D_INNER + 2 * SSM_GROUPS * SSM_STATE
SSM_IN_DIM = SSM_D_INNER + SSM_CONV_DIM + 2 * SSM_HEADS
D_FF = 4 * D_MODEL
NORM_EPS = 1e-6
NEG_INF = -1e30

kernel_name = "hybrid_na_ssd_prefix_dit_step"

def rms_norm(x, g):
    xf = x.astype(jnp.float32)
    y = xf * lax.rsqrt(jnp.mean(xf * xf, axis=-1, keepdims=True) + NORM_EPS)
    return (y * g.astype(jnp.float32)).astype(x.dtype)

def ada_mod(cond, w, b):
    m = jax.nn.silu(cond) @ w + b
    return jnp.split(m[:, None, :], 6, axis=-1)

def modulate(h, shift, scale):
    return h * (1 + scale) + shift

def qkv_heads(h, w_qkv):
    b, L, _ = h.shape
    qkv = (h @ w_qkv).reshape(b, L, 3, NA_HEADS, NA_HEAD_DIM)
    return qkv[:, :, 0], qkv[:, :, 1], qkv[:, :, 2]

def ctx_self_attention(q, k, v):
    b, L, h, d = q.shape
    nb = L // CTX_Q_BLOCK
    qb = jnp.moveaxis((q * d ** -0.5).reshape(b, nb, CTX_Q_BLOCK, h, d), 1, 0)

    def block(qi):
        s = jnp.einsum('bqhd,bkhd->bhqk', qi, k).astype(jnp.float32)
        p = jax.nn.softmax(s, axis=-1).astype(v.dtype)
        return jnp.einsum('bhqk,bkhd->bqhd', p, v)

    o = lax.map(block, qb)
    return jnp.moveaxis(o, 0, 1).reshape(b, L, h, d)

def neighborhood_attention(q, k, v, ck, cv, rpb):
    b, S, h, d = q.shape
    rows = S // GRID_W
    kr = min(WIN_ROWS_MAX, rows)
    ncb = GRID_W // Q_COL_BLOCK
    r_idx = jnp.arange(rows)
    row_start = jnp.clip(r_idx - kr // 2, 0, rows - kr)
    band_start = jnp.clip(jnp.arange(ncb) * Q_COL_BLOCK - WIN_COLS // 2, 0, GRID_W - K_COL_BAND)
    band_cols = band_start[:, None] + jnp.arange(K_COL_BAND)
    q_cols = jnp.arange(ncb)[:, None] * Q_COL_BLOCK + jnp.arange(Q_COL_BLOCK)
    win_start = jnp.clip(q_cols - WIN_COLS // 2, 0, GRID_W - WIN_COLS)
    kc = band_cols[:, None, :]
    col_ok = (kc >= win_start[..., None]) & (kc < win_start[..., None] + WIN_COLS)
    dcol_idx = jnp.clip(kc - q_cols[..., None], -(WIN_COLS - 1), WIN_COLS - 1) + WIN_COLS - 1
    col_bias = rpb[:, :, dcol_idx]

    kg = k.reshape(b, rows, GRID_W, h, d)
    vg = v.reshape(b, rows, GRID_W, h, d)
    qg = jnp.moveaxis((q * d ** -0.5).reshape(b, rows, ncb, Q_COL_BLOCK, h, d), 1, 0)

    def one_row(args):
        q_r, r, rs = args
        k_blk = jnp.take(lax.dynamic_slice_in_dim(kg, rs, kr, axis=1), band_cols, axis=2)
        v_blk = jnp.take(lax.dynamic_slice_in_dim(vg, rs, kr, axis=1), band_cols, axis=2)
        s_loc = jnp.einsum('bnqhd,bjnkhd->bnqhjk', q_r, k_blk).astype(jnp.float32)
        drow_idx = rs + jnp.arange(kr) - r + WIN_ROWS_MAX - 1
        bias = jnp.take(col_bias, drow_idx, axis=1).transpose(2, 3, 0, 1, 4)
        s_loc = jnp.where(col_ok[:, :, None, None, :], s_loc + bias.astype(jnp.float32), NEG_INF)
        s_ctx = jnp.einsum('bnqhd,bchd->bnqhc', q_r, ck).astype(jnp.float32)
        nloc = kr * K_COL_BAND
        s = jnp.concatenate([s_loc.reshape(b, ncb, Q_COL_BLOCK, h, nloc), s_ctx], axis=-1)
        p = jax.nn.softmax(s, axis=-1).astype(v.dtype)
        p_loc = p[..., :nloc].reshape(b, ncb, Q_COL_BLOCK, h, kr, K_COL_BAND)
        return (jnp.einsum('bnqhjk,bjnkhd->bnqhd', p_loc, v_blk)
                + jnp.einsum('bnqhc,bchd->bnqhd', p[..., nloc:], cv))

    o = lax.map(one_row, (qg, r_idx, row_start))
    return jnp.moveaxis(o, 0, 1).reshape(b, S, h, d)

def centred_dwconv(u, w, bias):
    K = w.shape[0]
    pad = K // 2
    y = lax.conv_general_dilated(u, w[:, None, :], window_strides=(1,), padding=[(pad, K - 1 - pad)],
                                 dimension_numbers=('NWC', 'WIO', 'NWC'), feature_group_count=u.shape[-1])
    return y + bias

def ssd_scan(x, dt, a, bm, cm, d_skip, h0):
    b, L, H, P = x.shape
    G, N = bm.shape[2], bm.shape[3]
    E = H // G
    Q = SSM_CHUNK
    nc = L // Q
    f32 = jnp.float32
    xc = x.reshape(b, nc, Q, G, E, P).astype(f32)
    dtc = dt.reshape(b, nc, Q, G, E).astype(f32)
    bc = bm.reshape(b, nc, Q, G, N).astype(f32)
    cc = cm.reshape(b, nc, Q, G, N).astype(f32)
    a_cum = jnp.cumsum(dtc * a.astype(f32).reshape(G, E), axis=2)
    seg = a_cum[:, :, :, None] - a_cum[:, :, None, :]
    lower = jnp.tril(jnp.ones((Q, Q), dtype=bool))[None, None, :, :, None, None]
    decay = jnp.exp(jnp.where(lower, seg, NEG_INF))
    cb = jnp.einsum('bclgn,bcsgn->bclsg', cc, bc)
    y_diag = jnp.einsum('bclsge,bcsgep->bclgep', cb[..., None] * decay * dtc[:, :, None], xc)
    decay_end = jnp.exp(a_cum[:, :, -1:] - a_cum)
    chunk_states = jnp.einsum('bcsgn,bcsge,bcsgep->bcgepn', bc, decay_end * dtc, xc)
    chunk_decay = jnp.exp(a_cum[:, :, -1])

    def step(hs, inp):
        s_c, d_c = inp
        return hs * d_c[..., None, None] + s_c, hs

    h_fin, h_prev = lax.scan(step, h0.reshape(b, G, E, P, N).astype(f32),
                             (jnp.moveaxis(chunk_states, 1, 0), jnp.moveaxis(chunk_decay, 1, 0)))
    h_prev = jnp.moveaxis(h_prev, 0, 1)
    y_off = jnp.einsum('bclgn,bcgepn,bclge->bclgep', cc, h_prev, jnp.exp(a_cum))
    y = y_diag + y_off + xc * d_skip.astype(f32).reshape(G, E, 1)
    return y.reshape(b, L, H, P).astype(x.dtype), h_fin.reshape(b, H, P, N).astype(x.dtype)

def ssd_mixer(h, w_in, conv_w, conv_b, dt_bias, a_log, d_skip, norm_g, w_out, h0):
    b, L, _ = h.shape
    proj = h @ w_in
    z = proj[..., :SSM_D_INNER]
    xbc = jax.nn.silu(centred_dwconv(proj[..., SSM_D_INNER:SSM_D_INNER + SSM_CONV_DIM], conv_w, conv_b))
    dt_raw = proj[..., SSM_D_INNER + SSM_CONV_DIM:].reshape(b, L, 2, SSM_HEADS)
    gn = SSM_GROUPS * SSM_STATE
    xs = xbc[..., :SSM_D_INNER].reshape(b, L, SSM_HEADS, SSM_HEAD_DIM)
    bm = xbc[..., SSM_D_INNER:SSM_D_INNER + gn].reshape(b, L, SSM_GROUPS, SSM_STATE)
    cm = xbc[..., SSM_D_INNER + gn:].reshape(b, L, SSM_GROUPS, SSM_STATE)
    dt = jax.nn.softplus(dt_raw.astype(jnp.float32) + dt_bias.astype(jnp.float32))
    a = -jnp.exp(a_log.astype(jnp.float32))
    y_f, h_f = ssd_scan(xs, dt[:, :, 0], a[0], bm, cm, d_skip[0], h0[:, 0])
    fl = lambda t: jnp.flip(t, axis=1)
    y_b, h_b = ssd_scan(fl(xs), fl(dt[:, :, 1]), a[1], fl(bm), fl(cm), d_skip[1], h0[:, 1])
    y = (y_f + fl(y_b)).reshape(b, L, SSM_D_INNER)
    y = rms_norm(y * jax.nn.silu(z), norm_g)
    return y @ w_out, jnp.stack([h_f, h_b], axis=1)

def setup_inputs(seed: int = 0) -> dict:
    key = jax.random.key(seed)
    ks = iter(jax.random.split(key, 40))
    f32 = jnp.float32
    n_attn = (DEPTH + 1) // 2
    n_ssm = DEPTH // 2
    nrm = lambda shape, s: jax.random.normal(next(ks), shape, f32) * s
    gain = lambda shape: 1.0 + nrm(shape, 0.02)
    dt0 = jnp.exp(jax.random.uniform(next(ks), (n_ssm, 2, SSM_HEADS), f32, math.log(1e-3), math.log(1e-1)))
    return {
        "x_prompt": nrm((BATCH, SEQ, D_MODEL), 1.0),
        "x_sample": nrm((DEC_BATCH, DEC_SEQ, D_MODEL), 1.0),
        "cache_attn_k": nrm((DEC_BATCH, n_attn, PAST_LEN, NA_HEADS, NA_HEAD_DIM), 1.0),
        "cache_attn_v": nrm((DEC_BATCH, n_attn, PAST_LEN, NA_HEADS, NA_HEAD_DIM), 1.0),
        "state_ssm": nrm((DEC_BATCH, n_ssm, 2, SSM_HEADS, SSM_HEAD_DIM, SSM_STATE), 0.3),
        "c": nrm((DEC_BATCH, D_MODEL), 1.0),
        "c_ctx": nrm((D_MODEL,), 1.0),
        "mod_w": nrm((DEPTH, D_MODEL, 6 * D_MODEL), 0.5 * D_MODEL ** -0.5),
        "mod_b": nrm((DEPTH, 6 * D_MODEL), 0.02),
        "norm_mix": gain((DEPTH, D_MODEL)),
        "norm_mlp": gain((DEPTH, D_MODEL)),
        "mlp_w1": nrm((DEPTH, D_MODEL, D_FF), D_MODEL ** -0.5),
        "mlp_w2": nrm((DEPTH, D_FF, D_MODEL), D_FF ** -0.5),
        "na_wqkv": nrm((n_attn, D_MODEL, 3 * D_MODEL), D_MODEL ** -0.5),
        "na_wo": nrm((n_attn, D_MODEL, D_MODEL), D_MODEL ** -0.5),
        "na_rpb": nrm((n_attn, NA_HEADS, 2 * WIN_ROWS_MAX - 1, 2 * WIN_COLS - 1), 0.1),
        "ssm_w_in": nrm((n_ssm, D_MODEL, SSM_IN_DIM), D_MODEL ** -0.5),
        "ssm_conv_w": nrm((n_ssm, SSM_CONV, SSM_CONV_DIM), SSM_CONV ** -0.5),
        "ssm_conv_b": nrm((n_ssm, SSM_CONV_DIM), 0.02),
        "ssm_dt_bias": dt0 + jnp.log(-jnp.expm1(-dt0)),
        "ssm_a_log": jnp.log(jax.random.uniform(next(ks), (n_ssm, 2, SSM_HEADS), f32, 1.0, 16.0)),
        "ssm_d": 1.0 + nrm((n_ssm, 2, SSM_HEADS), 0.1),
        "ssm_norm": gain((n_ssm, SSM_D_INNER)),
        "ssm_w_out": nrm((n_ssm, SSM_D_INNER, D_MODEL), SSM_D_INNER ** -0.5),
        "final_norm": gain((D_MODEL,)),
    }

def reference(x_prompt, x_sample, cache_attn_k, cache_attn_v, state_ssm, c, c_ctx, mod_w, mod_b,
              norm_mix, norm_mlp, mlp_w1, mlp_w2, na_wqkv, na_wo, na_rpb, ssm_w_in, ssm_conv_w,
              ssm_conv_b, ssm_dt_bias, ssm_a_log, ssm_d, ssm_norm, ssm_w_out, final_norm):
    xp, xs = x_prompt, x_sample
    bp, lp, _ = xp.shape
    bs, ls, _ = xs.shape
    new_k, new_v, new_ssm = [], [], []
    for i in range(DEPTH):
        j = i // N_MIXERS
        mp = ada_mod(c_ctx[None, :], mod_w[i], mod_b[i])
        ms = ada_mod(c, mod_w[i], mod_b[i])
        hp = modulate(rms_norm(xp, norm_mix[i]), mp[0], mp[1])
        hs = modulate(rms_norm(xs, norm_mix[i]), ms[0], ms[1])
        if i % N_MIXERS == 0:
            qp, kp, vp = qkv_heads(hp, na_wqkv[j])
            op = ctx_self_attention(qp, kp, vp).reshape(bp, lp, D_MODEL) @ na_wo[j]
            qs, ks_, vs = qkv_heads(hs, na_wqkv[j])
            os_ = neighborhood_attention(qs, ks_, vs, cache_attn_k[:, j], cache_attn_v[:, j],
                                         na_rpb[j]).reshape(bs, ls, D_MODEL) @ na_wo[j]
            new_k.append(kp)
            new_v.append(vp)
        else:
            h0 = jnp.zeros((bp, 2, SSM_HEADS, SSM_HEAD_DIM, SSM_STATE), xp.dtype)
            op, st = ssd_mixer(hp, ssm_w_in[j], ssm_conv_w[j], ssm_conv_b[j], ssm_dt_bias[j], ssm_a_log[j],
                               ssm_d[j], ssm_norm[j], ssm_w_out[j], h0)
            os_, _ = ssd_mixer(hs, ssm_w_in[j], ssm_conv_w[j], ssm_conv_b[j], ssm_dt_bias[j], ssm_a_log[j],
                               ssm_d[j], ssm_norm[j], ssm_w_out[j], state_ssm[:, j])
            new_ssm.append(st)
        xp = xp + mp[2] * op
        xs = xs + ms[2] * os_
        hp = modulate(rms_norm(xp, norm_mlp[i]), mp[3], mp[4])
        hs = modulate(rms_norm(xs, norm_mlp[i]), ms[3], ms[4])
        xp = xp + mp[5] * (jnp.square(jax.nn.relu(hp @ mlp_w1[i])) @ mlp_w2[i])
        xs = xs + ms[5] * (jnp.square(jax.nn.relu(hs @ mlp_w1[i])) @ mlp_w2[i])
    y_prompt = rms_norm(xp, final_norm)
    y_sample = rms_norm(xs, final_norm)
    new_attn_k = jnp.stack(new_k, axis=1)
    new_attn_v = jnp.stack(new_v, axis=1)
    new_ssm_state = jnp.stack(new_ssm, axis=1)
    return (y_prompt, y_sample, new_attn_k, new_attn_v, new_ssm_state)


_drawn_inputs = setup_inputs


def setup_inputs(seed=0):
    import zlib

    import numpy as np

    out = dict(_drawn_inputs(seed))
    spreads = {}
    factors = {'norm_mlp': 4.452, 'na_rpb': 8.0, 'ssm_d': 4.258, 'ssm_norm': 8.0, 'final_norm': 2.85}
    for name, (base, spread) in spreads.items():
        noise = np.random.default_rng([zlib.crc32(name.encode()), seed]).standard_normal(out[name].shape)
        drawn = base * np.exp(spread * noise) if base else spread * noise
        out[name] = __import__('jax').numpy.asarray(drawn.astype(out[name].dtype))
    for name, factor in factors.items():
        out[name] = (out[name] * factor).astype(out[name].dtype)
    return out
```

```python
from contextlib import ExitStack

import numpy as np
import concourse.bass as bass
from concourse import mybir

F32 = mybir.dt.float32
F32R = mybir.dt.float32r
ALU = mybir.AluOpType
ACT = mybir.ActivationFunctionType
AX = mybir.AxisListType

P = 128
D = 2048
KT = D // P
SEQ = 128
TOK = 2 * SEQ
HEADS = 16
GRID_W = 64
WIN_ROWS_MAX = 8
WIN_COLS = 16
DFF = 4 * D
D_INNER = 2 * D
SSM_HEADS = 64
SSM_GROUPS = 8
XT_TILES = D_INNER // P
XBC_TILES = XT_TILES + 2 * SSM_GROUPS
NORM_EPS = 1e-6
NEG = -1e30
CH_KT = 4
CH_N = 512
HALF = CH_KT // 2 * CH_N
RAW_SLOTS = 4
MOD_BLOCKS = 6 * KT
N_QUARTERS = DFF // D

PAT = {
    "M": [("M", q) for q in range(4)],
    "L": [("L", q) for q in range(4)],
    "LM": [(t, q) for q in range(4) for t in ("M", "L")],
}


class Phase:

    def __init__(self, name, kind, pat, n, w=None, k0=0, c0=0, mod=None, operand=None, width=CH_N, **more):
        self.name, self.kind, self.pat, self.n = name, kind, pat, n
        self.w, self.k0, self.c0, self.mod, self.operand, self.width = w, k0, c0, mod, operand, width
        self.more = more
        self.chunks = PAT[pat]
        self.m = len(self.chunks)


def layout(ins):
    (mod_w, w1, w2, wqkv, wo, w_in, w_out) = (ins[k] for k in (
        "mod_w", "mlp_w1", "mlp_w2", "na_wqkv", "na_wo", "ssm_w_in", "ssm_w_out"))
    ph = [Phase("mod", "mod", "M", 8, mod=(0, 0))]
    for j, kind in enumerate("qkv"):
        ph.append(Phase(kind, kind, "LM", 4, w=wqkv[0], c0=j * D, mod=(0, 8 + 4 * j), operand="HL"))
    ph.append(Phase("wo", "res", "LM", 4, w=wo[0], mod=(0, 20), operand="HID", layer=0, gate=2 * KT))
    for layer in range(2):
        if layer == 1:
            ph.append(Phase("dt", "dt", "L", 1, w=w_in[0], c0=D_INNER + XBC_TILES * P, operand="HL", width=P))
            ph.append(Phase("z", "z", "LM", 8, w=w_in[0], c0=0, mod=(1, 16), operand="HL"))
            ph.append(Phase("xbc", "xbc", "L", 12, w=w_in[0], c0=D_INNER, operand="HL"))
            for half in range(2):
                ph.append(Phase(f"wout{half}", "res", "L", 4, w=w_out[0], k0=half * KT,
                                operand=("HL", "HID")[half], layer=1, gate=2 * KT))
        for quarter in range(N_QUARTERS):
            ph.append(Phase(f"up{layer}_{quarter}", "w1", "L" if layer else "LM", 4, w=w1[layer], c0=quarter * D,
                            mod=None if layer else (1, 4 * quarter), operand="HL"))
            ph.append(Phase(f"down{layer}_{quarter}", "res", "L", 4, w=w2[layer], k0=quarter * KT,
                            operand="HID", layer=layer, gate=5 * KT))
    t = g = mg = 0
    for p in ph:
        p.T0, p.G0, p.M0 = t, g, mg
        t += p.m * p.n
        g += p.n if "L" in p.pat else 0
        mg += p.n if "M" in p.pat else 0
    return ph


def chunk_source(ins, p, col0, typ, q):
    if typ == "M":
        layer, g0 = p.mod
        view = ins["mod_w"][layer].rearrange("(t p) n -> p t n", p=P)
        return view[:, 4 * q:4 * q + 4, bass.ds(g0 * CH_N + col0, CH_N)]
    view = p.w.rearrange("(t p) n -> p t n", p=P)
    return view[:, p.k0 + 4 * q:p.k0 + 4 * q + 4, bass.ds(p.c0 + col0, p.width)]


def program(nc, ins, outs):
    ph = layout(ins)
    by_name = {p.name: p for p in ph}
    first_of = [p.T0 for p in ph]
    N_CHUNKS = ph[-1].T0 + ph[-1].m * ph[-1].n
    owner = [p for p in ph for _ in range(p.m * p.n)]

    def by_block(p, c):
        typ, q = p.chunks[c]
        return typ == "L" and (q == 3 or (q == 0 and p.pat == "L") or p.width < CH_N)

    def read_count(T, u):
        p = owner[T]
        return 4 * T + 4 if by_block(p, (T - p.T0) % p.m) else 4 * T + 2 * (u + 1)

    ctx = ExitStack()
    with ctx:
        base = (nc.sbuf_base + 31) // 32 * 32
        arena = ctx.enter_context(nc.sbuf_tensor("arena", [P, (nc.sbuf_usable_end - base - 64) // 4], F32))
        place = [base]

        def sb(name, shape, dt=F32, offset=None):
            at = place[0] if offset is None else offset
            size = 4
            for s in shape[1:]:
                size *= s
            if offset is None:
                place[0] = at + (size + 31) // 32 * 32
                assert place[0] <= nc.sbuf_usable_end - 32, (name, place[0])
            return nc.alloc_sbuf_tensor_at(name, shape, dt, offset=at)

        def sem(name):
            return ctx.enter_context(nc.semaphore(name))

        raw = sb("raw", [P, RAW_SLOTS, CH_KT * CH_N])
        w_hi = sb("w_hi", [P, 2, CH_KT * CH_N], F32R)
        w_lo = sb("w_lo", [P, 2, CH_KT * CH_N], F32R)
        X = sb("X", [P, KT, TOK])
        at_HL = place[0]
        HL = sb("HL", [P, KT, 2 * TOK], F32R)
        at_HID = place[0]
        HID = sb("HID", [P, KT, 2 * TOK], F32R)
        at_R = place[0]
        ROOM = sb("ROOM", [P, XBC_TILES, TOK])
        U = sb("U", [P, 4, TOK])
        PAR = sb("PAR", [P, 5, P])
        ident = sb("ident", [P, P])
        flip = sb("flip", [P, P])
        tri = sb("tri", [P, 2, P])
        modv = sb("modv", [P, 2, MOD_BLOCKS, 2])
        cond_w = sb("cond_w", [P, KT * 4 + P - 4], F32R)
        cond = cond_w[:, 0:KT * 4].rearrange("p (t v) -> p t v", v=4)
        modA = sb("modA", [P, KT, 2])
        rbc = sb("rbc", [P, TOK])
        m_rows = sb("m_rows", [4, CH_N])
        dt_tok = sb("dt_tok", [P, 2, P])
        ac_tok = sb("ac_tok", [P, 2, P])
        w_end = sb("w_end", [P, P])
        d_sum = sb("d_sum", [P, XT_TILES])
        col = sb("col", [P, 4])
        one = sb("one", [P, 1])
        comb = sb("comb", [4, 2])
        x_tok = sb("x_tok", [P, 2, D], offset=at_R)
        SQ = sb("SQ", [P, KT, TOK], offset=at_R + 16384)
        rows = sb("rows", [P, 5, P], offset=at_R + 32768)
        d_all = sb("d_all", [P, 2, SSM_HEADS], offset=at_R + 36864)
        win = sb("win", [P, 2, P], offset=at_R + 38912)
        csil = sb("csil", [P, 2, KT], offset=at_R + 40960)
        biasm = sb("biasm", [P, HEADS, P], offset=at_HID + 24576)
        qT = sb("qT", [P, KT, TOK], offset=at_R)
        kT = sb("kT", [P, KT, TOK], offset=at_R + 16384)
        vT = sb("vT", [P, KT, TOK], offset=at_R + 32768)
        ck = sb("ck", [P, D], offset=at_HL)
        cv = sb("cv", [P, D], offset=at_HL + 8192)
        v_tok = sb("v_tok", [P, 2, D], offset=at_HL + 16384)
        k_tok = sb("k_tok", [P, D], offset=at_R + 32768)
        prob = sb("prob", [P, 2, 384], offset=at_R + 40960)
        probT = sb("probT", [P, 2, 384], offset=at_R + 40960 + 3072)
        ckT = sb("ckT", [P, 2, P], offset=at_R + 40960 + 6144)
        smax = sb("smax", [P, 2, 2], offset=at_R + 40960 + 7168)
        ssum = sb("ssum", [P, 2, 2], offset=at_R + 40960 + 7200)
        zS = sb("zS", [P, XT_TILES, TOK], offset=at_HID)
        bc = sb("bc", [P, 2, 8, P], offset=at_HL)
        cbm = sb("cbm", [P, 2, 2, P], offset=at_HL + 8192)
        xd = sb("xd", [P, 3, 2, 512], offset=at_HL + 10240)
        h0T = sb("h0T", [P, 2, 512], offset=at_HL + 22528)
        ea = sb("ea", [P, 2, 4, P], offset=at_HL + 26624)
        s_out = sb("s_out", [P, 4, P], offset=at_HL + 30720)
        s_in = U
        b_tok = rbc
        y_tok = sb("y_tok", [P, 2, D], offset=at_R)

        bank = [ctx.enter_context(nc.psum_tensor(f"bank{i}", [P, 512], F32)) for i in range(8)]
        STAT, MCOL, MROW = bank[5], bank[6], bank[7]

        ac_dram = nc.dram_tensor("ac_scratch", (P, TOK), F32, kind="Internal").ap()

        raw_in = [sem(f"raw_in{i}") for i in range(RAW_SLOTS)]
        hi_ready = sem("hi_ready")
        lo_ready = sem("lo_ready")
        w_read = sem("w_read")
        evac = sem("evac")
        bank_free = sem("bank_free")
        group_out = sem("group_out")
        e2_step = sem("e2_step")
        silu_out = sem("silu_out")
        m_rows_in = sem("m_rows_in")
        m_cols = sem("m_cols")
        mod_out = sem("mod_out")
        cin = sem("cin")
        rin = sem("rin")
        xin = sem("xin")
        bin_ = sem("bin_")
        gin = sem("gin")
        act_step, dve_step = sem("act_step"), sem("dve_step")
        par_t, par_in = sem("par_t"), sem("par_in")
        cond_in = sem("cond_in")
        x_t, x_in = sem("x_t"), sem("x_in")
        init = sem("init")
        sq_ready, stat_ready, rms_root = sem("sq_ready"), sem("stat_ready"), sem("rms_root")
        scaled, oper_hi, oper = sem("scaled"), sem("oper_hi"), sem("oper")
        kv_in = sem("kv_in")
        vt_t, vt_in = sem("vt_t"), sem("vt_in")
        kvout = sem("kvout")
        ck_t, ck_in = sem("ck_t"), sem("ck_in")
        sc_ready, mx_ready, ex_ready, pr_ready = sem("sc_ready"), sem("mx_ready"), sem("ex_ready"), sem("pr_ready")
        pt_t, pt_in, o_ready = sem("pt_t"), sem("pt_in"), sem("o_ready")
        dt_a, dt_v, dt_t, dt_p, ac_w = sem("dt_a"), sem("dt_v"), sem("dt_t"), sem("dt_p"), sem("ac_w")
        fr_t, cb_ready, xd_ready, h0_in, bt_in = (sem(n) for n in ("fr_t", "cb_ready", "xd_ready", "h0_in", "bt_in"))
        si_in = sem("si_in")
        bc_in = [sem("bc_in0"), sem("bc_in1")]
        ea_in = sem("ea_in")
        seg_v, seg_a, dec_ready, mm_ready = (sem(n) for n in ("seg_v", "seg_a", "dec_ready", "mm_ready"))
        ea_ready, unit_pe, st_pe, st_sb, st_done = (sem(n) for n in ("ea_ready", "unit_pe", "st_pe", "st_sb", "st_done"))
        yo_pe, y_sb = sem("yo_pe"), sem("y_sb")
        yz, ysq, ysq_pe, y_root, y_sc, y_hi, y_op = (sem(n) for n in ("yz", "ysq", "ysq_pe", "y_root", "y_sc", "y_hi", "y_op"))
        f_sc, f_t, f_sb, f_done = (sem(n) for n in ("f_sc", "f_t", "f_sb", "f_done"))

        G_END = {p.name: p.G0 + p.n for p in ph if "L" in p.pat}
        block = ctx.enter_context(nc.Block())

        def runs(eng, p, body, peel=True):
            if p.n <= 2:
                for i in range(p.n):
                    body(i, 0)
                return
            body(0, 0)
            if p.n == 3:
                body(1, 0)
            else:
                with eng.Fori(0, p.n - 2) as s:
                    body(1, s)
            body(p.n - 1, 0)

        @block.sync
        def _(sp):
            for p in ph:
                def body(rep, shift, p=p):
                    free, col0 = [], rep * p.width
                    if not isinstance(shift, int):
                        free = [sp.snap(2 * (p.T0 + rep * p.m + c - RAW_SLOTS + 1) + shift * (2 * p.m))
                                for c in range(p.m)]
                        col0 = sp.snap(rep * p.width + shift * p.width)
                    for c, (typ, q) in enumerate(p.chunks):
                        T = p.T0 + rep * p.m + c
                        if T >= RAW_SLOTS:
                            sp.wait_ge(lo_ready, free[c] if free else 2 * (T - RAW_SLOTS + 1))
                        n = p.width if typ == "L" else CH_N
                        dst = raw[:, T % RAW_SLOTS, 0:CH_KT * n].rearrange("p (t n) -> p t n", t=CH_KT)
                        sp.dma_start(dst, chunk_source(ins, p, col0, typ, q)).then_inc(raw_in[T % RAW_SLOTS], 16)
                runs(sp, p, body)

        @block.gpsimd
        def _(pool):
            c = ins["consts"]
            pool.dma_start(ident[:, :], c[:, 0, :]).then_inc(cin, 16)
            pool.dma_start(comb[:, :], c[0:4, 5, 0:2]).then_inc(cin, 16)
            pool.dma_start(flip[:, :], c[:, 6, :]).then_inc(gin, 16)
            as_rows = lambda a: a.rearrange("(r p) -> r p", p=P)
            row_sets = [
                [(ins["mod_b"][0], 0, 96), (ins["c_ctx"], 96, 16), (ins["c"][0], 112, 16)],
                [(ins["mod_b"][1], 0, 96), (ins["norm_mix"][0], 96, 16), (ins["norm_mix"][1], 112, 16)],
                [(ins["ssm_conv_w"][0, 0], 0, 48), (ins["ssm_conv_w"][0, 1], 48, 48),
                 (ins["norm_mlp"][0], 96, 16), (ins["norm_mlp"][1], 112, 16)],
                [(ins["ssm_conv_w"][0, 2], 0, 48), (ins["ssm_conv_b"][0], 48, 48), (ins["ssm_norm"][0], 96, 32)],
                [(ins["final_norm"], 0, 16)],
            ]
            for s, parts in enumerate(row_sets):
                for a, r0, n in parts:
                    pool.dma_start(rows[r0:r0 + n, s, :], as_rows(a)).then_inc(rin, 16)
            pool.dma_start(x_tok[:, 0, :], ins["x_prompt"][0]).then_inc(xin, 16)
            pool.dma_start(x_tok[:, 1, :], ins["x_sample"][0]).then_inc(xin, 16)
            pool.dma_start(tri[:, :, :], c[:, 1:3, :]).then_inc(gin, 16)
            pool.dma_start(win[:, :, :], c[:, 3:5, :]).then_inc(gin, 16)
            pool.dma_start(d_all[:, :, :], ins["ssm_d"][0:1].to_broadcast([P, 2, SSM_HEADS])).then_inc(gin, 16)
            pool.dma_start(col[:, 0:1], ins["ssm_dt_bias"][0].rearrange("d (h o) -> (d h) o", o=1)).then_inc(gin, 16)
            pool.dma_start(col[:, 1:2], ins["ssm_a_log"][0].rearrange("d (h o) -> (d h) o", o=1)).then_inc(gin, 16)
            rpb = ins["na_rpb"]
            NC, NR = 2 * WIN_COLS - 1, 2 * WIN_ROWS_MAX - 1
            for rq in range(2):
                for rk in range(2):
                    src = bass.AP(rpb.tensor, (rk - rq + WIN_ROWS_MAX - 1) * NC + WIN_COLS - 1 - (GRID_W - 1),
                                  [[1, GRID_W], [NR * NC, HEADS], [1, GRID_W]])
                    pool.dma_start(biasm[rq * GRID_W:(rq + 1) * GRID_W, :, rk * GRID_W:(rk + 1) * GRID_W],
                                   src).then_inc(bin_, 16)

            pool.wait_ge(w_read, 4 * (by_name["wo"].T0))
            pool.dma_start(ck[:, :], ins["cache_attn_k"][0, 0].rearrange("t h d -> t (h d)")).then_inc(kv_in, 16)
            pool.dma_start(cv[:, :], ins["cache_attn_v"][0, 0].rearrange("t h d -> t (h d)")).then_inc(kv_in, 16)
            pool.wait_ge(vt_in, 8)
            pool.dma_start(outs["new_v"][0, 0].rearrange("t h d -> t (h d)"), v_tok[:, 0, :]).then_inc(kvout, 16)
            pool.wait_ge(vt_in, 12)
            pool.dma_start(outs["new_k"][0, 0].rearrange("t h d -> t (h d)"), k_tok[:, :]).then_inc(kvout, 16)
            pool.wait_ge(kvout, 32)
            pool.wait_ge(dt_p, 2)
            pool.dma_start(ac_dram, ROOM[:, 10, :]).then_inc(ac_w, 16)
            pool.wait_ge(ac_w, 16)
            state = ins["state_ssm"][0, 0].rearrange("d (b h) p n -> d (h p) b n", h=2)
            new_state = outs["new_state"][0, 0].rearrange("d (b h) p n -> d (h p) b n", h=2)
            pool.wait_ge(group_out, G_END["xbc"])
            pool.wait_ge(w_read, 4 * by_name["wout0"].T0)
            ac_v = ac_dram.rearrange("(d h) t -> d h t", d=2)

            def load_states(g):
                if g:
                    pool.wait_ge(fr_t, 2 * g)
                for d in range(2):
                    pool.dma_start(s_in[:, :, d * P:(d + 1) * P], state[d, :, 4 * g:4 * g + 4, :]).then_inc(si_in, 16)

            def load_unit(u):
                g, r, d = u // 4, u // 2 % 2, u % 2
                if u >= 2:
                    pool.wait_ge(unit_pe, u - 1)
                pool.dma_start(bc[:, d, :, :], ac_v[d:d + 1, 8 * g:8 * g + 8, r * SEQ:(r + 1) * SEQ]
                               .to_broadcast([P, 8, SEQ])).then_inc(bc_in[d], 16)

            def load_ea(g):
                if g:
                    pool.wait_ge(y_sb, 2 * g)
                for d in range(2):
                    for h in range(2):
                        src = ac_v[d:d + 1, 8 * g + h:8 * g + 8:2, SEQ:].to_broadcast([64, 4, SEQ])
                        pool.dma_start(ea[64 * h:64 * h + 64, d, :, :], src).then_inc(ea_in, 16)

            load_states(0)
            load_unit(0)
            load_unit(1)
            for g in range(SSM_GROUPS):
                load_ea(g)
                load_unit(4 * g + 2)
                load_unit(4 * g + 3)
                for d in range(2):
                    pool.wait_ge(st_sb, 2 * g + d + 1)
                    pool.dma_start(new_state[d, :, 4 * g:4 * g + 4, :], s_out[:, :, :]).then_inc(st_done, 16)
                if g + 1 < SSM_GROUPS:
                    load_states(g + 1)
                    load_unit(4 * g + 4)
                    load_unit(4 * g + 5)
            pool.wait_ge(st_done, 16 * 2 * SSM_GROUPS)
            for r, name in enumerate(("y_prompt", "y_sample")):
                pool.wait_ge(f_sb, 8)
                pool.dma_start(outs[name][0], y_tok[:, r, :]).then_inc(f_done, 16)
            pool.wait_ge(f_done, 32)

        @block.scalar
        def _(act):
            asteps = [0]

            def link(i):
                asteps[0] += 1
                i.then_inc(act_step, 1)
                act.wait_ge(act_step, asteps[0])

            def split(T, rate, shift):
                p = owner[T]
                typ, _q = p.chunks[(T - p.T0) % p.m]
                n = HALF if typ == "M" else CH_KT // 2 * p.width
                for u in range(2):
                    if u == 0:
                        act.wait_ge(raw_in[T % RAW_SLOTS], 16 * (T // RAW_SLOTS + 1) + shift * (4 * rate))
                    if T >= 2:
                        act.wait_ge(w_read, read_count(T - 2, u) + shift * (4 * rate))
                    nc.scalar.activation(w_hi[:, T % 2, u * n:(u + 1) * n], raw[:, T % RAW_SLOTS, u * n:(u + 1) * n],
                                         ACT.Copy).then_inc(hi_ready, 1)

            def phase(k):
                p = ph[k]

                def silu(rep, shift):
                    gi = p.G0 + rep
                    act.wait_ge(group_out, gi + 1 + shift)
                    dst = zS if p.kind == "z" else ROOM
                    v = dst[:, bass.ds(4 * rep + 4 * shift, 4), :]
                    nc.scalar.activation(v, v, ACT.Silu).then_inc(silu_out, 1)

                def body(rep, shift):
                    last = rep == p.n - 1
                    for c in range(1, p.m):
                        split(p.T0 + rep * p.m + c, p.m, shift)
                    if p.kind in ("z", "xbc") and rep:
                        silu(rep - 1, shift)
                    nxt = p.T0 + (rep + 1) * p.m
                    if nxt < N_CHUNKS:
                        split(nxt, p.m, shift)
                    if "M" in p.pat:
                        mg = p.M0 + rep
                        last_m = p.T0 + rep * p.m + max(c for c in range(p.m) if p.chunks[c][0] == "M")
                        act.wait_ge(w_read, 4 * (last_m + 1) + shift * (4 * p.m))
                        if mg:
                            act.wait_ge(m_cols, mg + shift)
                        nc.scalar.activation(m_rows[:, :], MROW[0:4, :], ACT.Copy).then_inc(m_rows_in, 1)
                    if "L" in p.pat:
                        gi = p.G0 + rep
                        for b in range(p.width // P):
                            done = 4 * (p.T0 + rep * p.m + p.m - 1) + (b + 1 if p.width == CH_N else 4)
                            act.wait_ge(w_read, done + shift * (4 * p.m))
                            if gi:
                                act.wait_ge(group_out, gi + shift)
                            i = nc.scalar.activation(U[:, b, :], bank[b][:, TOK:2 * TOK], ACT.Copy)
                            i.then_inc(evac, 1 if p.width == CH_N else 4)
                    if last and p.kind in ("z", "xbc"):
                        silu(rep, 0)
                runs(act, p, body)

            def norm_squares():
                for t in range(4):
                    nc.scalar.activation(SQ[:, 4 * t:4 * t + 4, :], X[:, 4 * t:4 * t + 4, :],
                                         ACT.Square).then_inc(sq_ready, 1)

            norms = [0]

            def norm_root():
                norms[0] += 1
                act.wait_ge(stat_ready, norms[0])
                act.wait_ge(init, 1)
                nc.scalar.activation(rbc[:, :], STAT[:, 0:TOK], ACT.Sqrt, scale=1.0 / D,
                                     bias=col[:, 3:4]).then_inc(rms_root, 1)

            def norm(g_done):
                if g_done is not None:
                    act.wait_ge(group_out, g_done)
                norm_squares()
                norm_root()
                n0 = 4 * (norms[0] - 1)
                for t in range(4):
                    act.wait_ge(scaled, n0 + t + 1)
                    nc.scalar.activation(HL[:, 4 * t:4 * t + 4, 0:TOK], SQ[:, 4 * t:4 * t + 4, :],
                                         ACT.Copy).then_inc(oper_hi, 1)

            act.wait_ge(par_in, 1)
            nc.scalar.activation(csil[:, :, :], PAR[:, 0, 96:128].rearrange("p (v t) -> p v t", v=2),
                                 ACT.Silu).then_inc(cond_in, 1)
            act.wait_ge(cond_in, 1)
            nc.scalar.activation(cond[:, :, 0:2], csil[:, :, :].rearrange("p v t -> p t v"),
                                 ACT.Copy).then_inc(cond_in, 1)
            split(0, 4, 0)
            phase(0)
            act.wait_ge(x_in, 8)
            norm(None)
            phase(1)
            phase(2)
            phase(3)

            def copy_out(n, dst, src, semaphore):
                nc.scalar.activation(dst, src, ACT.Copy).then_inc(semaphore, 1)

            for j in range(8):
                act.wait_ge(vt_t, j + 1)
                nc.scalar.activation(v_tok[:, :, 2 * j * P:(2 * j + 2) * P].rearrange("p g (t d) -> p t g d", t=2),
                                     bank[j % 4][:, :].rearrange("p (t g d) -> p t g d", t=2, g=2),
                                     ACT.Copy).then_inc(vt_in, 1)
            for j in range(4):
                act.wait_ge(vt_t, 8 + j + 1)
                nc.scalar.activation(k_tok[:, 4 * j * P:(4 * j + 4) * P], bank[j % 4][:, :], ACT.Copy).then_inc(vt_in, 1)

            def a_ckT(h):
                act.wait_ge(ck_t, h + 1)
                nc.scalar.activation(ckT[:, h % 2, :], bank[h % 2][:, 384:512], ACT.Copy).then_inc(ck_in, 1)

            def a_exp(h):
                act.wait_ge(mx_ready, h + 1)
                if h >= 2:
                    act.wait_ge(pt_t, h - 1)
                nc.scalar.activation(prob[:, h % 2, 0:128], bank[h % 2][:, 0:128], ACT.Exp,
                                     bias=smax[:, h % 2, 0:1], accum_out=ssum[:, h % 2, 0:1])
                nc.scalar.activation(prob[:, h % 2, 128:384], bank[h % 2][:, 128:384], ACT.Exp,
                                     bias=smax[:, h % 2, 1:2], accum_out=ssum[:, h % 2, 1:2]).then_inc(ex_ready, 1)

            def a_probT(h):
                act.wait_ge(pt_t, h + 1)
                nc.scalar.activation(probT[:, h % 2, :], bank[2 + h % 2][:, 0:384], ACT.Copy).then_inc(pt_in, 1)

            a_ckT(0)
            for s in range(HEADS + 1):
                if s < HEADS:
                    a_exp(s)
                if 1 <= s:
                    a_probT(s - 1)
                if s + 1 < HEADS:
                    a_ckT(s + 1)

            phase(4)
            act.wait_ge(kvout, 32)
            norm(G_END["wo"])
            for k in range(5, 13):
                phase(k)
            norm(G_END["down0_3"])
            phase(13)
            R = lambda j: ROOM[:, j, :]
            act.wait_ge(group_out, G_END["dt"])
            link(nc.scalar.activation(R(1), R(0), ACT.Abs))
            nc.scalar.activation(R(2), R(1), ACT.Exp, scale=-1.0).then_inc(dt_a, 1)
            nc.scalar.activation(col[:, 2:3], col[:, 1:2], ACT.Exp).then_inc(dt_a, 1)
            act.wait_ge(dt_v, 1)
            nc.scalar.activation(R(4), R(3), ACT.Ln).then_inc(dt_a, 1)
            phase(14)
            act.wait_ge(dt_t, 1)
            nc.scalar.activation(dt_tok[:, :, :], bank[4][:, 0:256].rearrange("p (r c) -> p r c", r=2), ACT.Copy)
            nc.scalar.activation(ROOM[:, 9, :], bank[4][:, 256:512], ACT.Copy).then_inc(dt_p, 1)
            act.wait_ge(dt_t, 2)
            nc.scalar.activation(ROOM[:, 10, :], bank[5][:, 0:256], ACT.Copy).then_inc(dt_p, 1)
            act.wait_ge(dt_t, 3)
            nc.scalar.activation(ac_tok[:, :, :], bank[4][:, 0:256].rearrange("p (r c) -> p r c", r=2),
                                 ACT.Copy).then_inc(dt_p, 1)
            act.wait_ge(dt_v, 4)
            nc.scalar.activation(ROOM[:, 12, 0:128], ROOM[:, 11, 0:128], ACT.Exp).then_inc(dt_a, 1)
            phase(15)

            for g in range(SSM_GROUPS):
                act.wait_ge(fr_t, 2 * g + 2)
                for d in range(2):
                    nc.scalar.activation(h0T[:, d, :], bank[6 + d][:, :], ACT.Copy).then_inc(h0_in, 1)
                act.wait_ge(ea_in, 64 * (g + 1))
                nc.scalar.activation(ea[:, :, :, :], ea[:, :, :, :], ACT.Exp).then_inc(ea_ready, 1)
                for r in range(2):
                    for d in range(2):
                        u = 4 * g + 2 * r + d
                        if r == 0:
                            act.wait_ge(seg_v, u // 4 * 2 + d + 1)
                            nc.scalar.activation(bc[:, d, :, :], bc[:, d, :, :], ACT.Exp).then_inc(dec_ready, 1)
                        else:
                            act.wait_ge(bc_in[d], 16 * (2 * g + 2))
                            for e in range(8):
                                hd = d * SSM_HEADS + 8 * g + e
                                i = nc.scalar.activation(bc[:, d, e, :], bc[:, d, e, :], ACT.Relu, scale=-1.0,
                                                         bias=ac_tok[:, 1, hd:hd + 1])
                            i.then_inc(seg_a, 1)
                            act.wait_ge(seg_a, 2 * g + d + 1)
                            nc.scalar.activation(bc[:, d, :, :], bc[:, d, :, :], ACT.Exp,
                                                 scale=-1.0).then_inc(dec_ready, 1)
                    if r == 0:
                        for d in range(2):
                            act.wait_ge(st_pe, 2 * g + d + 1)
                            if 2 * g + d:
                                act.wait_ge(st_done, 16 * (2 * g + d))
                            nc.scalar.activation(s_out[:, :, :], bank[5][:, :].rearrange("p (b n) -> p b n", b=4),
                                                 ACT.Copy).then_inc(st_sb, 1)

            for t in range(8):
                act.wait_ge(yz, t + 1)
                if t >= 4:
                    act.wait_ge(ysq_pe, t - 3)
                nc.scalar.activation(ROOM[:, 32 + 4 * (t % 4):36 + 4 * (t % 4), :], ROOM[:, 4 * t:4 * t + 4, :],
                                     ACT.Square).then_inc(ysq, 1)
            act.wait_ge(ysq_pe, 8)
            act.wait_ge(st_done, 16 * 2 * SSM_GROUPS)
            nc.scalar.activation(rbc[:, :], STAT[:, 0:TOK], ACT.Sqrt, scale=1.0 / D_INNER,
                                 bias=col[:, 3:4]).then_inc(y_root, 1)
            for t in range(8):
                act.wait_ge(y_sc, t + 1)
                dst = (HL, HID)[t // 4]
                nc.scalar.activation(dst[:, 4 * (t % 4):4 * (t % 4) + 4, 0:TOK], ROOM[:, 4 * t:4 * t + 4, :],
                                     ACT.Copy).then_inc(y_hi, 1)
            phase(16)
            phase(17)
            norm(G_END["wout1"])
            for k in range(18, 26):
                phase(k)
            act.wait_ge(group_out, G_END["down1_3"])
            norm_squares()
            norm_root()
            for j in range(8):
                act.wait_ge(f_t, j + 1)
                nc.scalar.activation(y_tok[:, :, 2 * j * P:(2 * j + 2) * P].rearrange("p g (t d) -> p t g d", t=2),
                                     bank[j % 4][:, :].rearrange("p (t g d) -> p t g d", t=2, g=2),
                                     ACT.Copy).then_inc(f_sb, 1)

        @block.vector
        def _(dve):
            dsteps = [0]
            e2 = [0]

            def link(i):
                dsteps[0] += 1
                i.then_inc(dve_step, 1)
                dve.wait_ge(dve_step, dsteps[0])

            def split(T, rate, shift):
                p = owner[T]
                typ, _q = p.chunks[(T - p.T0) % p.m]
                n = HALF if typ == "M" else CH_KT // 2 * p.width
                for u in range(2):
                    dve.wait_ge(hi_ready, 2 * T + u + 1 + shift * (2 * rate))
                    s = slice(u * n, (u + 1) * n)
                    nc.vector.tensor_tensor(w_lo[:, T % 2, s], raw[:, T % RAW_SLOTS, s], w_hi[:, T % 2, s],
                                            ALU.subtract).then_inc(lo_ready, 1)

            E2_STEPS = {"w1": 2, "xbc": 2}

            def phase(k):
                p = ph[k]
                steps = E2_STEPS.get(p.kind, 0)
                e2_0 = e2[0]
                e2[0] += steps * p.n

                def finish(rep, shift):
                    gi = p.G0 + rep
                    dve.wait_ge(bank_free, 4 * (gi + 2) + 4 * shift)
                    tiles = bass.ds(4 * rep + 4 * shift, 4)
                    Uall = U[:, :, :]

                    def step(i, s):
                        i.then_inc(e2_step, 1)
                        dve.wait_ge(e2_step, e2_0 + steps * rep + s + steps * shift)
                    if p.kind in "qkv":
                        dst = {"q": qT, "k": kT, "v": vT}[p.kind]
                        i = nc.vector.tensor_scalar(dst[:, tiles, :], Uall, float(P) ** -0.5 if p.kind == "q" else 1.0,
                                                    None, ALU.mult)
                    elif p.kind == "z":
                        i = nc.vector.tensor_copy(zS[:, tiles, :], Uall)
                    elif p.kind == "dt":
                        i = nc.vector.tensor_scalar(ROOM[:, 0, :], U[:, 0, :], col[:, 0:1], None, ALU.add)
                    elif p.kind == "w1":
                        step(nc.vector.scalar_tensor_tensor(Uall, Uall, 0.0, Uall, ALU.max, ALU.mult), 1)
                        step(nc.vector.tensor_copy(HID[:, tiles, 0:TOK], Uall), 2)
                        i = nc.vector.tensor_tensor(HID[:, tiles, TOK:2 * TOK], Uall, HID[:, tiles, 0:TOK],
                                                    ALU.subtract)
                    elif p.kind == "res":
                        layer, gate = p.more["layer"], p.more["gate"]
                        for b in range(4):
                            for r in range(2):
                                xt = X[:, bass.ds(4 * rep + b + 4 * shift, 1), r * SEQ:(r + 1) * SEQ].rearrange("p o t -> p (o t)")
                                gt = modv[:, layer, bass.ds(gate + 4 * rep + b + 4 * shift, 1), r]
                                i = nc.vector.scalar_tensor_tensor(xt, U[:, b, r * SEQ:(r + 1) * SEQ], gt, xt,
                                                                   ALU.mult, ALU.add)
                    elif p.kind == "xbc":
                        def par(s, r0, b):
                            return PAR[:, s, bass.ds(r0 + 4 * rep + b + 4 * shift, 1)]
                        for b in range(4):
                            o = ROOM[:, bass.ds(4 * rep + b + 4 * shift, 1), :].rearrange("p o t -> p (o t)")
                            i = nc.vector.tensor_scalar(o, U[:, b, :], par(2, 48, b), par(3, 48, b), ALU.mult, ALU.add)
                        step(i, 1)
                        for b in range(4):
                            o = ROOM[:, bass.ds(4 * rep + b + 4 * shift, 1), :].rearrange("p o (r t) -> p (o r) t", r=2)
                            u = U[:, b, :].rearrange("p (r t) -> p r t", r=2)
                            i = nc.vector.scalar_tensor_tensor(o[:, :, 1:SEQ], u[:, :, 0:SEQ - 1], par(2, 0, b),
                                                               o[:, :, 1:SEQ], ALU.mult, ALU.add)
                        step(i, 2)
                        for b in range(4):
                            o = ROOM[:, bass.ds(4 * rep + b + 4 * shift, 1), :].rearrange("p o (r t) -> p (o r) t", r=2)
                            u = U[:, b, :].rearrange("p (r t) -> p r t", r=2)
                            i = nc.vector.scalar_tensor_tensor(o[:, :, 0:SEQ - 1], u[:, :, 1:SEQ], par(3, 0, b),
                                                               o[:, :, 0:SEQ - 1], ALU.mult, ALU.add)
                    i.then_inc(group_out, 1)

                def mod_bias(rep, shift):
                    mg = p.M0 + rep
                    layer, g0 = p.mod
                    dve.wait_ge(m_cols, mg + 1 + shift)
                    first = 4 * (g0 + rep)
                    bias = PAR[:, layer, bass.ds(first + 4 * shift, 4)].unsqueeze(2).to_broadcast([P, 4, 2])
                    nc.vector.tensor_tensor(modv[:, layer, bass.ds(first + 4 * shift, 4), :],
                                            MCOL[:, 0:8].rearrange("p (b v) -> p b v", b=4), bias,
                                            ALU.add).then_inc(mod_out, 1)

                def body(rep, shift):
                    split(p.T0 + rep * p.m + 1, p.m, shift)
                    if rep and "L" in p.pat:
                        finish(rep - 1, shift)
                    if rep and "M" in p.pat:
                        mod_bias(rep - 1, shift)
                    for c in range(2, p.m):
                        split(p.T0 + rep * p.m + c, p.m, shift)
                    nxt = p.T0 + (rep + 1) * p.m
                    if nxt < N_CHUNKS:
                        split(nxt, p.m, shift)
                    if "L" in p.pat:
                        gi = p.G0 + rep
                        for b in range(p.width // P):
                            dve.wait_ge(evac, 4 * gi + (b + 1 if p.width == CH_N else 4) + 4 * shift)
                            i = nc.vector.tensor_tensor(U[:, b, :], bank[b][:, 0:TOK], U[:, b, :], ALU.add)
                            i.then_inc(bank_free, 1 if p.width == CH_N else 4)
                    if rep == p.n - 1:
                        if "L" in p.pat:
                            finish(rep, 0)
                        if "M" in p.pat:
                            mod_bias(rep, 0)
                runs(dve, p, body)

            norms = [0]

            def norm(layer, scale, shift_, gain, last=False):
                k = norms[0]
                norms[0] += 1
                if not last:
                    dve.wait_ge(mod_out, 1 + max(p.M0 + p.n for p in ph if "M" in p.pat and p.T0 < cur[0]))
                    g = gain.unsqueeze(2).to_broadcast([P, KT, 2])
                    link(nc.vector.scalar_tensor_tensor(modA[:, :, :], modv[:, layer, scale:scale + KT, :], 1.0, g,
                                                        ALU.add, ALU.mult))
                dve.wait_ge(rms_root, k + 1)
                link(nc.vector.reciprocal(rbc[:, :], rbc[:, :]))
                r4 = rbc[:, :].unsqueeze(1).to_broadcast([P, 4, TOK])

                def lo(t):
                    dve.wait_ge(oper_hi, 4 * k + t + 1)
                    s = slice(4 * t, 4 * t + 4)
                    nc.vector.tensor_tensor(HL[:, s, TOK:2 * TOK], SQ[:, s, :], HL[:, s, 0:TOK],
                                            ALU.subtract).then_inc(oper, 1)
                for t in range(4):
                    s = slice(4 * t, 4 * t + 4)
                    link(nc.vector.tensor_tensor(SQ[:, s, :], X[:, s, :], r4, ALU.mult))
                    if last:
                        g4 = gain[:, s].unsqueeze(2).to_broadcast([P, 4, TOK])
                        nc.vector.tensor_tensor(SQ[:, s, :], SQ[:, s, :], g4, ALU.mult).then_inc(f_sc, 1)
                        continue
                    v = SQ[:, s, :].rearrange("p t (r c) -> p (t r) c", r=2)
                    a = modA[:, s, :].rearrange("p t r -> p (t r)").unsqueeze(2).to_broadcast([P, 8, SEQ])
                    b = modv[:, layer, shift_ + 4 * t:shift_ + 4 * t + 4, :].rearrange("p t r -> p (t r)") \
                        .unsqueeze(2).to_broadcast([P, 8, SEQ])
                    link(nc.vector.tensor_tensor(v, v, a, ALU.mult))
                    nc.vector.tensor_tensor(v, v, b, ALU.add).then_inc(scaled, 1)
                    if t:
                        lo(t - 1)
                if not last:
                    lo(3)

            cur = [0]

            dve.sem_inc(bank_free, 4)
            dve.sem_inc(mod_out, 1)
            nc.vector.memset(col[:, 3:4], NORM_EPS)
            nc.vector.memset(cond_w[:, KT * 4:].bitcast(F32), 0.0)
            nc.vector.memset(one[:, :], 1.0).then_inc(init, 1)
            dve.wait_ge(par_t, 1)
            nc.vector.tensor_copy(PAR[:, 0:4, :], bank[0][:, :].rearrange("p (s c) -> p s c", s=4)).then_inc(par_in, 1)
            dve.wait_ge(par_t, 2)
            nc.vector.tensor_copy(PAR[:, 4, 0:16], bank[1][:, 0:16]).then_inc(par_in, 1)
            dve.wait_ge(cond_in, 2)
            nc.vector.tensor_tensor(cond[:, :, 2:4], csil[:, :, :].rearrange("p v t -> p t v"), cond[:, :, 0:2],
                                    ALU.subtract).then_inc(cond_in, 1)
            split(0, 4, 0)
            for j in range(8):
                dve.wait_ge(x_t, j + 1)
                nc.vector.tensor_copy(X[:, 2 * j:2 * j + 2, :],
                                      bank[2 + j % 4][:, :].rearrange("p (t c) -> p t c", t=2)).then_inc(x_in, 1)
            dve.wait_ge(gin, 96)
            for h in range(2):
                q = slice(64 * h, 64 * h + 64)
                nc.vector.tensor_tensor(d_sum[q, :], d_all[q, 0, h::2], d_all[q, 1, h::2], ALU.add)
            dve.wait_ge(bin_, 64)
            keep = win[:, 0:1, :].to_broadcast([P, HEADS, P])
            neg = win[:, 1:2, :].to_broadcast([P, HEADS, P])
            link(nc.vector.tensor_tensor(biasm[:, :, :], biasm[:, :, :], keep, ALU.mult))
            link(nc.vector.tensor_tensor(biasm[:, :, :], biasm[:, :, :], neg, ALU.add))
            phase(0)
            dve.wait_ge(x_in, 8)
            cur[0] = ph[1].T0
            norm(0, KT, 0, PAR[:, 1, 96:112])
            phase(1)
            phase(2)
            phase(3)

            def d_max(h):
                dve.wait_ge(sc_ready, h + 1)
                nc.vector.reduce_max(smax[:, h % 2, 0:1], bank[h % 2][:, 0:128], AX.X, negate=True)
                nc.vector.reduce_max(smax[:, h % 2, 1:2], bank[h % 2][:, 128:384], AX.X,
                                     negate=True).then_inc(mx_ready, 1)

            def d_norm(h):
                dve.wait_ge(ex_ready, h + 1)
                link(nc.vector.reciprocal(ssum[:, h % 2, :], ssum[:, h % 2, :]))
                nc.vector.tensor_scalar(prob[:, h % 2, 0:128], prob[:, h % 2, 0:128], ssum[:, h % 2, 0:1], None, ALU.mult)
                nc.vector.tensor_scalar(prob[:, h % 2, 128:384], prob[:, h % 2, 128:384], ssum[:, h % 2, 1:2], None,
                                        ALU.mult).then_inc(pr_ready, 1)

            def d_out(h):
                dve.wait_ge(o_ready, h + 1)
                link(nc.vector.tensor_copy(HID[:, h, 0:TOK], bank[4 + h % 2][:, 0:TOK]))
                nc.vector.tensor_tensor(HID[:, h, TOK:2 * TOK], bank[4 + h % 2][:, 0:TOK], HID[:, h, 0:TOK],
                                        ALU.subtract).then_inc(oper, 1)

            for s in range(HEADS + 2):
                if s < HEADS:
                    d_max(s)
                if s >= 2:
                    d_out(s - 2)
                if s < HEADS:
                    d_norm(s)

            phase(4)
            dve.wait_ge(kvout, 32)
            cur[0] = ph[5].T0
            norm(0, 4 * KT, 3 * KT, PAR[:, 2, 96:112])
            for k in range(5, 13):
                phase(k)
            cur[0] = ph[13].T0
            norm(1, KT, 0, PAR[:, 1, 112:128])
            phase(13)
            R = lambda j: ROOM[:, j, :]
            dve.wait_ge(dt_a, 1)
            nc.vector.tensor_scalar(R(3), R(2), 1.0, None, ALU.add).then_inc(dt_v, 1)
            dve.wait_ge(dt_v, 1)
            link(nc.vector.tensor_scalar(R(5), R(3), 1.0, None, ALU.subtract))
            link(nc.vector.tensor_tensor(R(5), R(5), R(2), ALU.subtract))
            link(nc.vector.reciprocal(R(6), R(3)))
            link(nc.vector.tensor_tensor(R(5), R(5), R(6), ALU.mult))
            dve.wait_ge(dt_a, 3)
            link(nc.vector.tensor_tensor(R(4), R(4), R(5), ALU.subtract))
            link(nc.vector.scalar_tensor_tensor(R(7), R(0), 0.0, R(4), ALU.max, ALU.add))
            nc.vector.tensor_scalar(R(8), R(7), col[:, 2:3], -1.0, ALU.mult, ALU.mult).then_inc(dt_v, 1)
            phase(14)
            dve.wait_ge(dt_t, 4)
            dve.wait_ge(dt_p, 3)
            dve.wait_ge(group_out, G_END["z"])
            nc.vector.tensor_tensor(ROOM[:, 11, 0:128], bank[5][:, 256:384], ac_tok[:, 0, :], ALU.subtract).then_inc(dt_v, 1)
            dve.sem_inc(dt_v, 1)
            dve.wait_ge(dt_a, 4)
            link(nc.vector.tensor_tensor(w_end[:, :], ROOM[:, 12, 0:128], dt_tok[:, 0, :], ALU.mult))
            dve.wait_ge(ac_w, 16)
            phase(15)

            for g in range(SSM_GROUPS):
                dve.wait_ge(fr_t, 2 * g + 2)
                if g:
                    dve.wait_ge(unit_pe, 4 * g)
                    dve.wait_ge(st_pe, 2 * g)
                for r in range(2):
                    for d in range(2):
                        i = nc.vector.tensor_tensor(cbm[:, r, d, :], bank[2][:, r * P:(r + 1) * P], tri[:, d, :], ALU.mult)
                i.then_inc(cb_ready, 1)
                nc.vector.tensor_copy(b_tok[:, 0:128], bank[2][:, 256:384]).then_inc(bt_in, 1)
                for kind in range(3):
                    for d in range(2):
                        r = kind % 2
                        hd = d * SSM_HEADS + 8 * g
                        w = (w_end[:, hd:hd + 8] if kind == 2 else dt_tok[:, r, hd:hd + 8]).unsqueeze(2).to_broadcast([P, 8, 64])
                        i = nc.vector.tensor_tensor(xd[:, kind, d, :].rearrange("p (h c) -> p h c", h=8),
                                                    bank[r][:, :].rearrange("p (h c) -> p h c", h=8), w, ALU.mult)
                i.then_inc(xd_ready, 1)
                for r in range(2):
                    if r == 0:
                        for d in range(2):
                            dve.wait_ge(bc_in[d], 16 * (2 * g + 1))
                            for e in range(8):
                                hd = d * SSM_HEADS + 8 * g + e
                                i = nc.vector.tensor_scalar(bc[:, d, e, :], bc[:, d, e, :], ac_tok[:, 0, hd:hd + 1],
                                                            0.0, ALU.subtract, ALU.min)
                            i.then_inc(seg_v, 1)
                    if r == 0:
                        dve.wait_ge(cb_ready, g + 1)
                    for d in range(2):
                        u = 4 * g + 2 * r + d
                        dve.wait_ge(dec_ready, u + 1)
                        m = cbm[:, r, d:d + 1, :].to_broadcast([P, 8, P])
                        nc.vector.tensor_tensor(bc[:, d, :, :], bc[:, d, :, :], m, ALU.mult).then_inc(mm_ready, 1)
                    if r == 1:
                        for d in range(2):
                            dve.wait_ge(yo_pe, 2 * g + d + 1)
                            dve.wait_ge(ea_ready, g + 1)
                            i = nc.vector.tensor_tensor(ea[:, d, :, :], ea[:, d, :, :],
                                                        bank[6 + d][:, :].rearrange("p (b l) -> p b l", b=4), ALU.mult)
                        link(i)
                    dve.wait_ge(unit_pe, 4 * g + 2 * r + 2)
                    for j in range(4):
                        xt = ROOM[:, 4 * g + j, r * SEQ:(r + 1) * SEQ]
                        i = nc.vector.scalar_tensor_tensor(xt, xt, d_sum[:, 4 * g + j:4 * g + j + 1],
                                                           bank[3 + r][:, j * P:(j + 1) * P], ALU.mult, ALU.add)
                    if r == 1:
                        xa = ROOM[:, 4 * g:4 * g + 4, SEQ:]
                        link(i)
                        link(nc.vector.tensor_tensor(xa, xa, ea[:, 0, :, :], ALU.add))
                        i = nc.vector.tensor_tensor(xa, xa, ea[:, 1, :, :], ALU.add)
                    i.then_inc(y_sb, 1)

            for t in range(8):
                dve.wait_ge(silu_out, 20)
                dve.wait_ge(y_sb, 16)
                s = slice(4 * t, 4 * t + 4)
                nc.vector.tensor_tensor(ROOM[:, s, :], ROOM[:, s, :], zS[:, s, :], ALU.mult).then_inc(yz, 1)
            dve.wait_ge(yz, 8)
            dve.wait_ge(y_root, 1)
            dve.wait_ge(st_done, 16 * 2 * SSM_GROUPS)
            link(nc.vector.reciprocal(rbc[:, :], rbc[:, :]))
            r4 = rbc[:, :].unsqueeze(1).to_broadcast([P, 4, TOK])

            def y_lo(t):
                dve.wait_ge(y_hi, t + 1)
                dst = (HL, HID)[t // 4]
                s = slice(4 * (t % 4), 4 * (t % 4) + 4)
                nc.vector.tensor_tensor(dst[:, s, TOK:2 * TOK], ROOM[:, 4 * t:4 * t + 4, :], dst[:, s, 0:TOK],
                                        ALU.subtract).then_inc(y_op, 1)
            for t in range(8):
                s = slice(4 * t, 4 * t + 4)
                link(nc.vector.tensor_tensor(ROOM[:, s, :], ROOM[:, s, :], r4, ALU.mult))
                g4 = PAR[:, 3, 96 + 4 * t:100 + 4 * t].unsqueeze(2).to_broadcast([P, 4, TOK])
                nc.vector.tensor_tensor(ROOM[:, s, :], ROOM[:, s, :], g4, ALU.mult).then_inc(y_sc, 1)
                if t:
                    y_lo(t - 1)
            y_lo(7)
            phase(16)
            phase(17)
            cur[0] = ph[18].T0
            norm(1, 4 * KT, 3 * KT, PAR[:, 2, 112:128])
            for k in range(18, 26):
                phase(k)
            norm(1, 0, 0, PAR[:, 4, 0:16], last=True)

        @block.tensor
        def _(pe):
            def phase(k, ready):
                p = ph[k]
                A = {"HL": HL, "HID": HID, None: None}[p.operand]
                nb = p.width // P

                def body(s):
                    for c, (typ, q) in enumerate(p.chunks):
                        T = p.T0 + c
                        slot = T % 2
                        if typ == "M":
                            for u in range(2):
                                pe.wait_ge(lo_ready, 2 * T + u + 1 + s * (2 * p.m))
                                for kk in range(2):
                                    kt = 2 * u + kk
                                    at = 4 * (4 * q + kt)
                                    lhs = cond_w[:, at:at + P]
                                    for part, w in enumerate((w_hi, w_lo)):
                                        first = q == 0 and kt == 0 and part == 0
                                        last = q == 3 and kt == 3 and part == 1
                                        i = nc.tensor.matmul(MROW[:, :], lhs, w[:, slot, kt * CH_N:(kt + 1) * CH_N],
                                                             start=first, stop=last)
                                i.then_inc(w_read, 2)
                            continue
                        n = p.width
                        sem_, value = ready(q)
                        pe.wait_ge(sem_, value)
                        block_order = by_block(p, c)

                        def products(b, kts):
                            for kt in kts:
                                hi = w_hi[:, slot, kt * n + b * P:kt * n + (b + 1) * P]
                                lo = w_lo[:, slot, kt * n + b * P:kt * n + (b + 1) * P]
                                first, last = q == 0 and kt == 0, q == 3 and kt == 3
                                a = A[:, 4 * q + kt, :]
                                if not first:
                                    nc.tensor.matmul(bank[b][:, 0:TOK], lo, a[:, 0:TOK], start=False, stop=False)
                                i = nc.tensor.matmul(bank[b][:, :], hi, a, start=first, stop=last)
                                if first:
                                    i = nc.tensor.matmul(bank[b][:, 0:TOK], lo, a[:, 0:TOK], start=False, stop=False)
                            return i

                        def bank_wait(b):
                            if q == 0:
                                pe.wait_ge(bank_free, 4 * p.G0 + b + 1 + s * 4)
                        if block_order:
                            pe.wait_ge(lo_ready, 2 * T + 2 + s * (2 * p.m))
                            for b in range(nb):
                                bank_wait(b)
                                products(b, range(4)).then_inc(w_read, 4 // nb)
                        else:
                            for u in range(2):
                                pe.wait_ge(lo_ready, 2 * T + u + 1 + s * (2 * p.m))
                                for b in range(nb):
                                    if u == 0:
                                        bank_wait(b)
                                    i = products(b, (2 * u, 2 * u + 1))
                                i.then_inc(w_read, 2)
                    if "M" in p.pat:
                        pe.wait_ge(m_rows_in, p.M0 + 1 + s)
                        pe.wait_ge(mod_out, p.M0 + 1 + s)
                        for b in range(4):
                            i = nc.tensor.matmul(MCOL[:, 2 * b:2 * b + 2], m_rows[:, b * P:(b + 1) * P], comb[:, :],
                                                 start=True, stop=True)
                        i.then_inc(m_cols, 1)
                if p.n == 1:
                    body(0)
                else:
                    with pe.Fori(0, p.n) as s:
                        body(s)

            norms = [0]
            ones = one[:, 0:1].to_broadcast([P, P])

            def norm():
                for k in range(KT):
                    if k % 4 == 0:
                        pe.wait_ge(sq_ready, 4 * norms[0] + k // 4 + 1)
                    i = nc.tensor.matmul(STAT[:, 0:TOK], ones, SQ[:, k, :], start=k == 0, stop=k == KT - 1)
                i.then_inc(stat_ready, 1)
                norms[0] += 1

            pe.wait_ge(cin, 32)
            pe.wait_ge(rin, 16 * 14)
            for s in range(4):
                i = nc.tensor.transpose(bank[0][:, s * P:(s + 1) * P], rows[:, s, :], ident[:, :])
            i.then_inc(par_t, 1)
            nc.tensor.transpose(bank[1][:, 0:16], rows[0:16, 4, :], ident[0:16, 0:16]).then_inc(par_t, 1)
            pe.wait_ge(xin, 32)
            pe.wait_ge(init, 1)
            for j in range(8):
                if j >= 4:
                    pe.wait_ge(x_in, j - 3)
                for t in range(2):
                    for r in range(2):
                        f = (2 * j + t) * P
                        i = nc.tensor.transpose(bank[2 + j % 4][:, (2 * t + r) * P:(2 * t + r + 1) * P],
                                                x_tok[:, r, f:f + P], ident[:, :])
                i.then_inc(x_t, 1)
            pe.wait_ge(cond_in, 3)
            phase(0, None)
            norm()
            pe.wait_ge(rms_root, 1)
            for k in (1, 2, 3):
                phase(k, lambda q: (oper, q + 1))

            pe.wait_ge(group_out, G_END["v"])
            for j in range(8):
                if j < 4:
                    pe.wait_ge(bank_free, 4 * G_END["v"] + 4)
                else:
                    pe.wait_ge(vt_in, j - 3)
                for t in range(2):
                    for r in range(2):
                        i = nc.tensor.transpose(bank[j % 4][:, (2 * t + r) * P:(2 * t + r + 1) * P],
                                                vT[:, 2 * j + t, r * SEQ:(r + 1) * SEQ], ident[:, :])
                i.then_inc(vt_t, 1)
            for j in range(4):
                pe.wait_ge(vt_in, 5 + j)
                for t in range(4):
                    i = nc.tensor.transpose(bank[j % 4][:, t * P:(t + 1) * P], kT[:, 4 * j + t, 0:SEQ], ident[:, :])
                i.then_inc(vt_t, 1)
            pe.wait_ge(vt_in, 12)
            pe.wait_ge(kv_in, 32)

            def p_ckT(h):
                if h >= 2:
                    pe.wait_ge(ex_ready, h - 1)
                nc.tensor.transpose(bank[h % 2][:, 384:512], ck[:, h * P:(h + 1) * P], ident[:, :]).then_inc(ck_t, 1)

            def p_scores(h):
                pe.wait_ge(ck_in, h + 1)
                S = bank[h % 2]
                nc.tensor.matmul(S[:, 0:128], qT[:, h, 0:SEQ], kT[:, h, 0:SEQ], start=True, stop=True)
                nc.tensor.matmul(S[:, 128:256], flip[:, :], biasm[:, h, :], start=True, stop=False)
                nc.tensor.matmul(S[:, 128:256], qT[:, h, SEQ:], kT[:, h, SEQ:], start=False, stop=True)
                nc.tensor.matmul(S[:, 256:384], qT[:, h, SEQ:], ckT[:, h % 2, :], start=True, stop=True).then_inc(sc_ready, 1)

            def p_probT(h):
                pe.wait_ge(pr_ready, h + 1)
                if h >= 2:
                    pe.wait_ge(pt_in, h - 1)
                for j in range(3):
                    i = nc.tensor.transpose(bank[2 + h % 2][:, j * P:(j + 1) * P], prob[:, h % 2, j * P:(j + 1) * P], ident[:, :])
                i.then_inc(pt_t, 1)

            def p_out(h):
                pe.wait_ge(pt_in, h + 1)
                if h >= 2:
                    pe.wait_ge(oper, 4 + h - 1)
                O = bank[4 + h % 2]
                hs = slice(h * P, (h + 1) * P)
                nc.tensor.matmul(O[:, 0:128], v_tok[:, 0, hs], probT[:, h % 2, 0:128], start=True, stop=True)
                nc.tensor.matmul(O[:, 128:256], v_tok[:, 1, hs], probT[:, h % 2, 128:256], start=True, stop=False)
                nc.tensor.matmul(O[:, 128:256], cv[:, hs], probT[:, h % 2, 256:384], start=False, stop=True).then_inc(o_ready, 1)

            p_ckT(0)
            for s in range(HEADS + 2):
                if s < HEADS:
                    p_scores(s)
                if 1 <= s <= HEADS:
                    p_probT(s - 1)
                if s + 1 < HEADS:
                    p_ckT(s + 1)
                if s >= 2:
                    p_out(s - 2)

            phase(4, lambda q: (oper, 4 + 4 * (q + 1)))
            norm()
            base_op = [20]

            def mlp(k0):
                for q_ in range(N_QUARTERS):
                    phase(k0 + 2 * q_, lambda q, b=base_op[0]: (oper, b + q + 1))
                    phase(k0 + 2 * q_ + 1, lambda q, g=ph[k0 + 2 * q_].G0: (group_out, g + q + 1))
            mlp(5)
            norm()
            phase(13, lambda q: (oper, 24 + q + 1))
            phase(14, lambda q: (oper, 24 + q + 1))
            pe.wait_ge(dt_v, 2)
            pe.wait_ge(gin, 96)
            for n in range(2):
                for r in range(2):
                    i = nc.tensor.transpose(bank[4][:, (2 * n + r) * P:(2 * n + r + 1) * P],
                                            ROOM[:, 7 + n, r * SEQ:(r + 1) * SEQ], ident[:, :])
            i.then_inc(dt_t, 1)
            pe.wait_ge(dt_p, 1)
            for r in range(2):
                for d in range(2):
                    i = nc.tensor.matmul(bank[5][64 * d:64 * d + 64, r * SEQ:(r + 1) * SEQ],
                                         ROOM[:, 9, r * P + 64 * d:r * P + 64 * d + 64], tri[:, d, :], start=True, stop=True)
            i.then_inc(dt_t, 1)
            pe.wait_ge(dt_p, 2)
            for r in range(2):
                i = nc.tensor.transpose(bank[4][:, r * P:(r + 1) * P], ROOM[:, 10, r * SEQ:(r + 1) * SEQ], ident[:, :])
            i.then_inc(dt_t, 1)
            nc.tensor.matmul(bank[5][:, 256:384], ones, ROOM[:, 9, 0:P], start=True, stop=True).then_inc(dt_t, 1)
            phase(15, lambda q: (oper, 24 + q + 1))

            pe.wait_ge(bank_free, 4 * G_END["xbc"] + 4)
            pe.wait_ge(silu_out, 20)
            for g in range(SSM_GROUPS):
                Bt, Ct = ROOM[:, XT_TILES + g, :], ROOM[:, XT_TILES + SSM_GROUPS + g, :]
                if g:
                    pe.wait_ge(y_sb, 2 * g)
                    pe.wait_ge(st_sb, 2 * g)
                    pe.wait_ge(xd_ready, g)
                for r in range(2):
                    for j in range(4):
                        nc.tensor.transpose(bank[r][:, j * P:(j + 1) * P], ROOM[:, 4 * g + j, r * SEQ:(r + 1) * SEQ], ident[:, :])
                    nc.tensor.matmul(bank[2][:, r * P:(r + 1) * P], Bt[:, r * SEQ:(r + 1) * SEQ],
                                     Ct[:, r * SEQ:(r + 1) * SEQ], start=True, stop=True)
                nc.tensor.transpose(bank[2][:, 256:384], Bt[:, 0:SEQ], ident[:, :])
                pe.wait_ge(si_in, 32 * (g + 1))
                for d in range(2):
                    for j in range(4):
                        i = nc.tensor.transpose(bank[6 + d][:, j * P:(j + 1) * P], s_in[:, j, d * P:(d + 1) * P], ident[:, :])
                    i.then_inc(fr_t, 1)

                def unit(r, d):
                    u = 4 * g + 2 * r + d
                    pe.wait_ge(mm_ready, u + 1)
                    for e in range(8):
                        o = 64 * (e % 2)
                        i = nc.tensor.matmul(bank[3 + r][o:o + 64, (e // 2) * P:(e // 2 + 1) * P],
                                             xd[:, r, d, 64 * e:64 * e + 64], bc[:, d, e, :],
                                             start=d == 0 and e < 2, stop=d == 1, skip_group_check=True)
                    i.then_inc(unit_pe, 1)

                pe.wait_ge(xd_ready, g + 1)
                pe.wait_ge(bt_in, g + 1)
                for d in range(2):
                    if d:
                        pe.wait_ge(st_sb, 2 * g + 1)
                    for j in range(4):
                        i = nc.tensor.matmul(bank[5][:, j * P:(j + 1) * P], xd[:, 2, d, j * P:(j + 1) * P],
                                             b_tok[:, 0:P], start=True, stop=True)
                    i.then_inc(st_pe, 1)
                    if d == 0:
                        unit(0, 0)
                        unit(0, 1)
                for d in range(2):
                    pe.wait_ge(h0_in, 2 * g + 2)
                    for j in range(4):
                        i = nc.tensor.matmul(bank[6 + d][:, j * P:(j + 1) * P], h0T[:, d, j * P:(j + 1) * P],
                                             Ct[:, SEQ:], start=True, stop=True)
                    i.then_inc(yo_pe, 1)
                unit(1, 0)
                unit(1, 1)

            for t in range(8):
                pe.wait_ge(ysq, t + 1)
                for j in range(4):
                    i = nc.tensor.matmul(STAT[:, 0:TOK], ones, ROOM[:, 32 + 4 * (t % 4) + j, :],
                                         start=t == 0 and j == 0, stop=t == 7 and j == 3)
                i.then_inc(ysq_pe, 1)
            phase(16, lambda q: (y_op, q + 1))
            phase(17, lambda q: (y_op, 4 + q + 1))
            norm()
            base_op[0] = 28
            mlp(18)
            norm()
            for j in range(8):
                pe.wait_ge(f_sc, j // 2 + 1)
                if j < 4:
                    pe.wait_ge(bank_free, 4 * G_END["down1_3"] + 4)
                else:
                    pe.wait_ge(f_sb, j - 3)
                for t in range(2):
                    for r in range(2):
                        i = nc.tensor.transpose(bank[j % 4][:, (2 * t + r) * P:(2 * t + r + 1) * P],
                                                SQ[:, 2 * j + t, r * SEQ:(r + 1) * SEQ], ident[:, :])
                i.then_inc(f_t, 1)


_INS = ["x_prompt", "x_sample", "cache_attn_k", "cache_attn_v", "state_ssm", "c", "c_ctx", "mod_w", "mod_b",
        "norm_mix", "norm_mlp", "mlp_w1", "mlp_w2", "na_wqkv", "na_wo", "na_rpb", "ssm_w_in", "ssm_conv_w",
        "ssm_conv_b", "ssm_dt_bias", "ssm_a_log", "ssm_d", "ssm_norm", "ssm_w_out", "final_norm"]
_OUTS = [("y_prompt", (1, 128, 2048)), ("y_sample", (1, 128, 2048)), ("new_k", (1, 1, 128, 16, 128)),
         ("new_v", (1, 1, 128, 16, 128)), ("new_state", (1, 1, 2, 64, 64, 128))]


def constants():
    c = np.zeros((P, 7, P), np.float32)
    t = np.arange(P)
    c[:, 0] = np.eye(P)
    c[:, 1] = t[:, None] <= t[None, :]
    c[:, 2] = t[:, None] >= t[None, :]
    qc, kc = t[:, None] % GRID_W, t[None, :] % GRID_W
    start = np.clip(qc - WIN_COLS // 2, 0, GRID_W - WIN_COLS)
    ok = (kc >= start) & (kc < start + WIN_COLS)
    c[:, 6] = (t[:, None] // GRID_W == t[None, :] // GRID_W) & (qc == GRID_W - 1 - kc)
    turned = np.argmax(c[:, 6], 1)
    c[:, 3] = ok[turned]
    c[:, 4] = np.where(ok[turned], 0.0, NEG)
    c[[0, 1, 2, 3], 5, [0, 1, 0, 1]] = 1.0
    return c


def kernel(**inputs):
    import numpy as _np
    import concourse.bacc as _bacc
    from concourse import mybir as _mybir
    from concourse.bass_utils import run_bass_kernel_spmd as _run

    nc = _bacc.Bacc("TRN2", target_bir_lowering=False, num_devices=1, dynamic_dma_scratch_size=8192)
    arrays = {f"in_{name}": _np.ascontiguousarray(inputs[name]) for name in _INS}
    arrays["in_consts"] = constants()
    ins = {name[3:]: nc.dram_tensor(name, a.shape, _mybir.dt.from_np(a.dtype), kind="ExternalInput").ap()
           for name, a in arrays.items()}
    outs = {name: nc.dram_tensor(f"out_{name}", shape, _mybir.dt.float32, kind="ExternalOutput").ap()
            for name, shape in _OUTS}
    program(nc, ins, outs)
    r = _run(nc, [arrays], core_ids=[0])
    return tuple(r.results[0][f"out_{name}"] for name, _ in _OUTS)
```

```python
from contextlib import ExitStack

import numpy as np
import concourse.bass as bass
from concourse import mybir

F32 = mybir.dt.float32
F32R = mybir.dt.float32r
ALU = mybir.AluOpType
ACT = mybir.ActivationFunctionType
AX = mybir.AxisListType

P = 128
D = 2048
KT = D // P
SEQ = 128
TOK = 2 * SEQ
HEADS = 16
GRID_W = 64
WIN_ROWS_MAX = 8
WIN_COLS = 16
DFF = 4 * D
D_INNER = 2 * D
SSM_HEADS = 64
SSM_GROUPS = 8
XT_TILES = D_INNER // P
XBC_TILES = XT_TILES + 2 * SSM_GROUPS
NORM_EPS = 1e-6
NEG = -1e30
CH_KT = 4
CH_N = 512
HALF = CH_KT // 2 * CH_N
RAW_SLOTS = 4
MOD_BLOCKS = 6 * KT
N_QUARTERS = DFF // D

PAT = {
    "M": [("M", q) for q in range(4)],
    "L": [("L", q) for q in range(4)],
    "LM": [(t, q) for q in range(4) for t in ("M", "L")],
}


class Phase:

    def __init__(self, name, kind, pat, n, w=None, k0=0, c0=0, mod=None, operand=None, width=CH_N, **more):
        self.name, self.kind, self.pat, self.n = name, kind, pat, n
        self.w, self.k0, self.c0, self.mod, self.operand, self.width = w, k0, c0, mod, operand, width
        self.more = more
        self.chunks = PAT[pat]
        self.m = len(self.chunks)


def layout(ins):
    (mod_w, w1, w2, wqkv, wo, w_in, w_out) = (ins[k] for k in (
        "mod_w", "mlp_w1", "mlp_w2", "na_wqkv", "na_wo", "ssm_w_in", "ssm_w_out"))
    ph = [Phase("mod", "mod", "M", 8, mod=(0, 0))]
    for j, kind in enumerate("qkv"):
        ph.append(Phase(kind, kind, "LM", 4, w=wqkv[0], c0=j * D, mod=(0, 8 + 4 * j), operand="HL"))
    ph.append(Phase("wo", "res", "LM", 4, w=wo[0], mod=(0, 20), operand="HID", layer=0, gate=2 * KT))
    for layer in range(2):
        if layer == 1:
            ph.append(Phase("dt", "dt", "L", 1, w=w_in[0], c0=D_INNER + XBC_TILES * P, operand="HL", width=P))
            ph.append(Phase("z", "z", "LM", 8, w=w_in[0], c0=0, mod=(1, 16), operand="HL"))
            ph.append(Phase("xbc", "xbc", "L", 12, w=w_in[0], c0=D_INNER, operand="HL"))
            for half in range(2):
                ph.append(Phase(f"wout{half}", "res", "L", 4, w=w_out[0], k0=half * KT,
                                operand=("HL", "HID")[half], layer=1, gate=2 * KT))
        for quarter in range(N_QUARTERS):
            ph.append(Phase(f"up{layer}_{quarter}", "w1", "L" if layer else "LM", 4, w=w1[layer], c0=quarter * D,
                            mod=None if layer else (1, 4 * quarter), operand="HL"))
            ph.append(Phase(f"down{layer}_{quarter}", "res", "L", 4, w=w2[layer], k0=quarter * KT,
                            operand="HID", layer=layer, gate=5 * KT))
    t = g = mg = 0
    for p in ph:
        p.T0, p.G0, p.M0 = t, g, mg
        t += p.m * p.n
        g += p.n if "L" in p.pat else 0
        mg += p.n if "M" in p.pat else 0
    return ph


def chunk_source(ins, p, col0, typ, q):
    if typ == "M":
        layer, g0 = p.mod
        view = ins["mod_w"][layer].rearrange("(t p) n -> p t n", p=P)
        return view[:, 4 * q:4 * q + 4, bass.ds(g0 * CH_N + col0, CH_N)]
    view = p.w.rearrange("(t p) n -> p t n", p=P)
    return view[:, p.k0 + 4 * q:p.k0 + 4 * q + 4, bass.ds(p.c0 + col0, p.width)]


def program(nc, ins, outs):
    ph = layout(ins)
    by_name = {p.name: p for p in ph}
    N_CHUNKS = ph[-1].T0 + ph[-1].m * ph[-1].n
    owner = [p for p in ph for _ in range(p.m * p.n)]

    def by_block(p, c):
        typ, q = p.chunks[c]
        return typ == "L" and (q == 3 or (q == 0 and p.pat == "L") or p.width < CH_N)

    def read_count(T, u):
        p = owner[T]
        return 4 * T + 4 if by_block(p, (T - p.T0) % p.m) else 4 * T + 2 * (u + 1)

    ctx = ExitStack()
    with ctx:
        base = (nc.sbuf_base + 31) // 32 * 32
        arena = ctx.enter_context(nc.sbuf_tensor("arena", [P, (nc.sbuf_usable_end - base - 64) // 4], F32))
        place = [base]

        def sb(name, shape, dt=F32, offset=None):
            at = place[0] if offset is None else offset
            size = 4
            for s in shape[1:]:
                size *= s
            if offset is None:
                place[0] = at + (size + 31) // 32 * 32
                assert place[0] <= nc.sbuf_usable_end - 32, (name, place[0])
            return nc.alloc_sbuf_tensor_at(name, shape, dt, offset=at)

        def sem(name):
            return ctx.enter_context(nc.semaphore(name))

        raw = sb("raw", [P, RAW_SLOTS, CH_KT * CH_N])
        at_w_hi = place[0]
        w_hi = sb("w_hi", [P, 2, CH_KT * CH_N], F32R)
        w_lo = sb("w_lo", [P, 2, CH_KT * CH_N], F32R)
        X = sb("X", [P, KT, TOK])
        at_HL = place[0]
        HL = sb("HL", [P, KT, 2 * TOK], F32R)
        at_HID = place[0]
        HID = sb("HID", [P, KT, 2 * TOK], F32R)
        at_R = place[0]
        ROOM = sb("ROOM", [P, XBC_TILES, TOK])
        U = sb("U", [P, 4, TOK])
        PAR = sb("PAR", [P, 5, P])
        ident = sb("ident", [P, P])
        flip = sb("flip", [P, P])
        tri = sb("tri", [P, 2, P])
        modv = sb("modv", [P, 2, MOD_BLOCKS, 2])
        cond_w = sb("cond_w", [P, KT * 4 + P - 4], F32R)
        cond = cond_w[:, 0:KT * 4].rearrange("p (t v) -> p t v", v=4)
        modA = sb("modA", [P, KT, 2])
        rbc = sb("rbc", [P, TOK])
        m_rows = sb("m_rows", [4, CH_N])
        dt_tok = sb("dt_tok", [P, 2, P])
        ac_tok = sb("ac_tok", [P, 2, P])
        w_end = sb("w_end", [P, P])
        d_sum = sb("d_sum", [P, XT_TILES])
        col = sb("col", [P, 4])
        one = sb("one", [P, 1])
        comb = sb("comb", [4, 2])
        x_tok = sb("x_tok", [P, 2, D], offset=at_R)
        SQ = sb("SQ", [P, KT, TOK], offset=at_R + 16384)
        rows = sb("rows", [P, 5, P], offset=at_R + 32768)
        d_all = sb("d_all", [P, 2, SSM_HEADS], offset=at_R + 36864)
        win = sb("win", [P, 2, P], offset=at_R + 38912)
        csil = sb("csil", [P, 2, KT], offset=at_R + 40960)
        biasm = sb("biasm", [P, HEADS, P], offset=at_HID + 24576)
        qT = sb("qT", [P, KT, TOK], offset=at_R)
        kT = sb("kT", [P, KT, TOK], offset=at_R + 16384)
        vT = sb("vT", [P, KT, TOK], offset=at_R + 32768)
        ck = sb("ck", [P, D], offset=at_HL)
        cv = sb("cv", [P, D], offset=at_HL + 8192)
        v_tok = sb("v_tok", [P, 2, D], offset=at_HL + 16384)
        k_tok = sb("k_tok", [P, D], offset=at_R + 32768)
        prob = sb("prob", [P, 2, 384], offset=at_R + 40960)
        probT = sb("probT", [P, 2, 384], offset=at_R + 40960 + 3072)
        ckT = sb("ckT", [P, 2, P], offset=at_R + 40960 + 6144)
        smax = sb("smax", [P, 2, 2], offset=at_R + 40960 + 7168)
        ssum = sb("ssum", [P, 2, 2], offset=at_R + 40960 + 7200)
        zS = sb("zS", [P, XT_TILES, TOK], offset=at_HID)
        bc = [sb("bc_prompt", [P, 2, 8, P], offset=at_HL),
              sb("bc_sample", [P, 2, 8, P], offset=at_w_hi + 4 * CH_KT * CH_N)]
        cbm = sb("cbm", [P, 2, 2, P], offset=at_HL + 8192)
        xd = sb("xd", [P, 3, 2, 512], offset=at_HL + 10240)
        h0T = sb("h0T", [P, 2, 512], offset=at_HL + 22528)
        ea = sb("ea", [P, 2, 4, P], offset=at_HL + 26624)
        s_out = sb("s_out", [P, 4, P], offset=at_HL + 30720)
        s_in = U
        b_tok = rbc
        y_tok = sb("y_tok", [P, 2, D], offset=at_R)

        bank = [ctx.enter_context(nc.psum_tensor(f"bank{i}", [P, 512], F32)) for i in range(8)]
        STAT, MCOL, MROW = bank[5], bank[6], bank[7]

        ac_dram = nc.dram_tensor("ac_scratch", (P, TOK), F32, kind="Internal").ap()

        raw_in = [sem(f"raw_in{i}") for i in range(RAW_SLOTS)]
        hi_ready = sem("hi_ready")
        lo_ready = sem("lo_ready")
        w_read = sem("w_read")
        evac = sem("evac")
        bank_free = sem("bank_free")
        group_out = sem("group_out")
        e2_step = sem("e2_step")
        silu_out = sem("silu_out")
        m_rows_in = sem("m_rows_in")
        m_cols = sem("m_cols")
        mod_out = sem("mod_out")
        cin = sem("cin")
        rin = sem("rin")
        xin = sem("xin")
        bin_ = sem("bin_")
        gin = sem("gin")
        act_step, dve_step = sem("act_step"), sem("dve_step")
        par_t, par_in = sem("par_t"), sem("par_in")
        cond_in = sem("cond_in")
        x_t, x_in = sem("x_t"), sem("x_in")
        init = sem("init")
        sq_ready, stat_ready, rms_root = sem("sq_ready"), sem("stat_ready"), sem("rms_root")
        scaled, oper_hi, oper = sem("scaled"), sem("oper_hi"), sem("oper")
        kv_in = sem("kv_in")
        vt_t, vt_in = sem("vt_t"), sem("vt_in")
        kvout = sem("kvout")
        ck_t, ck_in = sem("ck_t"), sem("ck_in")
        sc_ready, mx_ready, ex_ready, pr_ready = sem("sc_ready"), sem("mx_ready"), sem("ex_ready"), sem("pr_ready")
        pt_t, pt_in, o_ready = sem("pt_t"), sem("pt_in"), sem("o_ready")
        dt_a, dt_v, dt_t, dt_p, ac_w = sem("dt_a"), sem("dt_v"), sem("dt_t"), sem("dt_p"), sem("ac_w")
        fr_t, cb_ready, xd_ready, h0_in, bt_in = (sem(n) for n in ("fr_t", "cb_ready", "xd_ready", "h0_in", "bt_in"))
        si_in = sem("si_in")
        bc_in = [[sem(f"bc_in{r}{d}") for d in range(2)] for r in range(2)]
        fx_t, ea_used = sem("fx_t"), sem("ea_used")
        ea_in = sem("ea_in")
        seg_v, seg_p, seg_a, dec_ready, mm_ready = (sem(n) for n in ("seg_v", "seg_p", "seg_a", "dec_ready", "mm_ready"))
        ea_ready, unit_pe, st_pe, st_sb, st_done = (sem(n) for n in ("ea_ready", "unit_pe", "st_pe", "st_sb", "st_done"))
        yo_pe, y_sb = sem("yo_pe"), sem("y_sb")
        yz, ysq, ysq_pe, y_root, y_sc, y_hi, y_op = (sem(n) for n in ("yz", "ysq", "ysq_pe", "y_root", "y_sc", "y_hi", "y_op"))
        f_sc, f_t, f_sb, f_done = (sem(n) for n in ("f_sc", "f_t", "f_sb", "f_done"))

        G_END = {p.name: p.G0 + p.n for p in ph if "L" in p.pat}
        block = ctx.enter_context(nc.Block())

        def runs(eng, p, body):
            if p.n <= 2:
                for i in range(p.n):
                    body(i, 0)
                return
            body(0, 0)
            if p.n == 3:
                body(1, 0)
            else:
                with eng.Fori(0, p.n - 2) as s:
                    body(1, s)
            body(p.n - 1, 0)

        def first_splits(p):
            if p.pat == "LM":
                return {0: ((), (2,)), 1: ((), (3, 4)), 2: ((), (5, 6)), 3: ((), (7,))}
            return {0: ((), ()), 1: ((), ()), 2: ((2,), ()), 3: ((3,), ())}

        after_norm = {1, 5, 13, 16, 18}

        @block.sync
        def _(sp):
            ac_v = ac_dram.rearrange("(d h) t -> d h t", d=2)

            def load_units(g, r):
                for d in range(2):
                    if g:
                        sp.wait_ge(unit_pe, 4 * (g - 1) + 2 * r + d + 1)
                    sp.dma_start(bc[r][:, d, :, :], ac_v[d:d + 1, 8 * g:8 * g + 8, r * SEQ:(r + 1) * SEQ]
                                   .to_broadcast([P, 8, SEQ])).then_inc(bc_in[r][d], 16)

            def load_ea(g):
                if g:
                    sp.wait_ge(y_sb, 2 * g)
                for d in range(2):
                    for h in range(2):
                        src = ac_v[d:d + 1, 8 * g + h:8 * g + 8:2, SEQ:].to_broadcast([64, 4, SEQ])
                        sp.dma_start(ea[64 * h:64 * h + 64, d, :, :], src).then_inc(ea_in, 16)

            def scan_loads():
                sp.wait_ge(ac_w, 16)
                sp.wait_ge(w_read, 4 * by_name["wout0"].T0)
                sp.wait_ge(group_out, G_END["xbc"])
                for g in range(SSM_GROUPS):
                    load_units(g, 0)
                    load_units(g, 1)
                    load_ea(g)

            for p in ph:
                def body(rep, shift, p=p):
                    free, col0 = [], rep * p.width
                    if not isinstance(shift, int):
                        free = [sp.snap(2 * (p.T0 + rep * p.m + c - RAW_SLOTS + 1) + shift * (2 * p.m))
                                for c in range(p.m)]
                        col0 = sp.snap(rep * p.width + shift * p.width)
                    for c, (typ, q) in enumerate(p.chunks):
                        T = p.T0 + rep * p.m + c
                        if T >= RAW_SLOTS:
                            sp.wait_ge(lo_ready, free[c] if free else 2 * (T - RAW_SLOTS + 1))
                        n = p.width if typ == "L" else CH_N
                        dst = raw[:, T % RAW_SLOTS, 0:CH_KT * n].rearrange("p (t n) -> p t n", t=CH_KT)
                        sp.dma_start(dst, chunk_source(ins, p, col0, typ, q)).then_inc(raw_in[T % RAW_SLOTS], 16)
                    if p.name == "wout0" and rep == 0:
                        scan_loads()
                runs(sp, p, body)

        @block.gpsimd
        def _(pool):
            c = ins["consts"]
            pool.dma_start(ident[:, :], c[:, 0, :]).then_inc(cin, 16)
            pool.dma_start(comb[:, :], c[0:4, 5, 0:2]).then_inc(cin, 16)
            pool.dma_start(flip[:, :], c[:, 6, :]).then_inc(gin, 16)
            as_rows = lambda a: a.rearrange("(r p) -> r p", p=P)
            row_sets = [
                [(ins["mod_b"][0], 0, 96), (ins["c_ctx"], 96, 16), (ins["c"][0], 112, 16)],
                [(ins["mod_b"][1], 0, 96), (ins["norm_mix"][0], 96, 16), (ins["norm_mix"][1], 112, 16)],
                [(ins["ssm_conv_w"][0, 0], 0, 48), (ins["ssm_conv_w"][0, 1], 48, 48),
                 (ins["norm_mlp"][0], 96, 16), (ins["norm_mlp"][1], 112, 16)],
                [(ins["ssm_conv_w"][0, 2], 0, 48), (ins["ssm_conv_b"][0], 48, 48), (ins["ssm_norm"][0], 96, 32)],
                [(ins["final_norm"], 0, 16)],
            ]
            for s, parts in enumerate(row_sets):
                for a, r0, n in parts:
                    pool.dma_start(rows[r0:r0 + n, s, :], as_rows(a)).then_inc(rin, 16)
            pool.dma_start(x_tok[:, 0, :], ins["x_prompt"][0]).then_inc(xin, 16)
            pool.dma_start(x_tok[:, 1, :], ins["x_sample"][0]).then_inc(xin, 16)
            pool.dma_start(tri[:, :, :], c[:, 1:3, :]).then_inc(gin, 16)
            pool.dma_start(win[:, :, :], c[:, 3:5, :]).then_inc(gin, 16)
            pool.dma_start(d_all[:, :, :], ins["ssm_d"][0:1].to_broadcast([P, 2, SSM_HEADS])).then_inc(gin, 16)
            pool.dma_start(col[:, 0:1], ins["ssm_dt_bias"][0].rearrange("d (h o) -> (d h) o", o=1)).then_inc(gin, 16)
            pool.dma_start(col[:, 1:2], ins["ssm_a_log"][0].rearrange("d (h o) -> (d h) o", o=1)).then_inc(gin, 16)
            rpb = ins["na_rpb"]
            NC, NR = 2 * WIN_COLS - 1, 2 * WIN_ROWS_MAX - 1
            for rq in range(2):
                for rk in range(2):
                    src = bass.AP(rpb.tensor, (rk - rq + WIN_ROWS_MAX - 1) * NC + WIN_COLS - 1 - (GRID_W - 1),
                                  [[1, GRID_W], [NR * NC, HEADS], [1, GRID_W]])
                    pool.dma_start(biasm[rq * GRID_W:(rq + 1) * GRID_W, :, rk * GRID_W:(rk + 1) * GRID_W],
                                   src).then_inc(bin_, 16)

            pool.wait_ge(w_read, 4 * (by_name["wo"].T0))
            pool.dma_start(ck[:, :], ins["cache_attn_k"][0, 0].rearrange("t h d -> t (h d)")).then_inc(kv_in, 16)
            pool.dma_start(cv[:, :], ins["cache_attn_v"][0, 0].rearrange("t h d -> t (h d)")).then_inc(kv_in, 16)
            pool.wait_ge(vt_in, 8)
            pool.dma_start(outs["new_v"][0, 0].rearrange("t h d -> t (h d)"), v_tok[:, 0, :]).then_inc(kvout, 16)
            pool.wait_ge(vt_in, 12)
            pool.dma_start(outs["new_k"][0, 0].rearrange("t h d -> t (h d)"), k_tok[:, :]).then_inc(kvout, 16)
            pool.wait_ge(kvout, 32)
            pool.wait_ge(dt_p, 2)
            pool.dma_start(ac_dram, ROOM[:, 10, :]).then_inc(ac_w, 16)
            pool.wait_ge(ac_w, 16)
            state = ins["state_ssm"][0, 0].rearrange("d (b h) p n -> d (h p) b n", h=2)
            new_state = outs["new_state"][0, 0].rearrange("d (b h) p n -> d (h p) b n", h=2)
            pool.wait_ge(group_out, G_END["xbc"])
            pool.wait_ge(w_read, 4 * by_name["wout0"].T0)
            def load_states(g):
                if g:
                    pool.wait_ge(fr_t, 2 * g)
                for d in range(2):
                    pool.dma_start(s_in[:, :, d * P:(d + 1) * P], state[d, :, 4 * g:4 * g + 4, :]).then_inc(si_in, 16)

            def store_state(g, d):
                pool.wait_ge(st_sb, 2 * g + d + 1)
                pool.dma_start(new_state[d, :, 4 * g:4 * g + 4, :], s_out[:, :, :]).then_inc(st_done, 16)

            load_states(0)
            for g in range(SSM_GROUPS):
                if g + 1 < SSM_GROUPS:
                    load_states(g + 1)
                store_state(g, 0)
                store_state(g, 1)
            pool.wait_ge(st_done, 16 * 2 * SSM_GROUPS)
            for r, name in enumerate(("y_prompt", "y_sample")):
                pool.wait_ge(f_sb, 8)
                pool.dma_start(outs[name][0], y_tok[:, r, :]).then_inc(f_done, 16)
            pool.wait_ge(f_done, 32)

        @block.scalar
        def _(act):
            asteps = [0]

            def link(i):
                asteps[0] += 1
                i.then_inc(act_step, 1)
                act.wait_ge(act_step, asteps[0])

            def split(T, rate, shift):
                p = owner[T]
                typ, _q = p.chunks[(T - p.T0) % p.m]
                n = HALF if typ == "M" else CH_KT // 2 * p.width
                for u in range(2):
                    if u == 0:
                        act.wait_ge(raw_in[T % RAW_SLOTS], 16 * (T // RAW_SLOTS + 1) + shift * (4 * rate))
                    if T >= 2:
                        act.wait_ge(w_read, read_count(T - 2, u) + shift * (4 * rate))
                    nc.scalar.activation(w_hi[:, T % 2, u * n:(u + 1) * n], raw[:, T % RAW_SLOTS, u * n:(u + 1) * n],
                                         ACT.Copy).then_inc(hi_ready, 1)

            def squares(batches):
                for t in batches:
                    nc.scalar.activation(SQ[:, 4 * t:4 * t + 4, :], X[:, 4 * t:4 * t + 4, :],
                                         ACT.Square).then_inc(sq_ready, 1)

            def phase(k, norm_next=False):
                p = ph[k]

                def silu(rep, shift):
                    gi = p.G0 + rep
                    act.wait_ge(group_out, gi + 1 + shift)
                    dst = zS if p.kind == "z" else ROOM
                    v = dst[:, bass.ds(4 * rep + 4 * shift, 4), :]
                    nc.scalar.activation(v, v, ACT.Silu).then_inc(silu_out, 1)

                def body(rep, shift):
                    last = rep == p.n - 1
                    for c in range(1, p.m):
                        if rep or k not in after_norm:
                            split(p.T0 + rep * p.m + c, p.m, shift)
                    if p.kind in ("z", "xbc") and rep:
                        silu(rep - 1, shift)
                    nxt = p.T0 + (rep + 1) * p.m
                    if nxt < N_CHUNKS:
                        split(nxt, p.m, shift)
                    if "M" in p.pat:
                        mg = p.M0 + rep
                        last_m = p.T0 + rep * p.m + max(c for c in range(p.m) if p.chunks[c][0] == "M")
                        act.wait_ge(w_read, 4 * (last_m + 1) + shift * (4 * p.m))
                        if mg:
                            act.wait_ge(m_cols, mg + shift)
                        nc.scalar.activation(m_rows[:, :], MROW[0:4, :], ACT.Copy).then_inc(m_rows_in, 1)
                    if last and norm_next:
                        act.wait_ge(group_out, p.G0 + rep)
                        squares(range(3))
                    if "L" in p.pat:
                        gi = p.G0 + rep
                        for b in range(p.width // P):
                            done = 4 * (p.T0 + rep * p.m + p.m - 1) + (b + 1 if p.width == CH_N else 4)
                            act.wait_ge(w_read, done + shift * (4 * p.m))
                            if gi:
                                act.wait_ge(group_out, gi + shift)
                            i = nc.scalar.activation(U[:, b, :], bank[b][:, TOK:2 * TOK], ACT.Copy)
                            i.then_inc(evac, 1 if p.width == CH_N else 4)
                    if last and p.kind in ("z", "xbc"):
                        silu(rep, 0)
                runs(act, p, body)

            norms = [0]

            def norm_root():
                norms[0] += 1
                act.wait_ge(stat_ready, norms[0])
                act.wait_ge(init, 1)
                nc.scalar.activation(rbc[:, :], STAT[:, 0:TOK], ACT.Sqrt, scale=1.0 / D,
                                     bias=col[:, 3:4]).then_inc(rms_root, 1)

            def norm(g_done, p):
                if g_done is not None:
                    act.wait_ge(group_out, g_done)
                squares(range(3, 4) if g_done is not None else range(4))
                split(p.T0 + 1, p.m, 0)
                norm_root()
                n0 = 4 * (norms[0] - 1)
                for t in range(4):
                    act.wait_ge(scaled, n0 + t + 1)
                    nc.scalar.activation(HL[:, 4 * t:4 * t + 4, 0:TOK], SQ[:, 4 * t:4 * t + 4, :],
                                         ACT.Copy).then_inc(oper_hi, 1)
                    for c in first_splits(p)[t][0] + first_splits(p)[t][1]:
                        split(p.T0 + c, p.m, 0)

            act.wait_ge(par_in, 1)
            nc.scalar.activation(csil[:, :, :], PAR[:, 0, 96:128].rearrange("p (v t) -> p v t", v=2),
                                 ACT.Silu).then_inc(cond_in, 1)
            act.wait_ge(cond_in, 1)
            nc.scalar.activation(cond[:, :, 0:2], csil[:, :, :].rearrange("p v t -> p t v"),
                                 ACT.Copy).then_inc(cond_in, 1)
            split(0, 4, 0)
            phase(0)
            act.wait_ge(x_in, 8)
            norm(None, ph[1])
            phase(1)
            phase(2)
            phase(3)

            for j in range(8):
                act.wait_ge(vt_t, j + 1)
                nc.scalar.activation(v_tok[:, :, 2 * j * P:(2 * j + 2) * P].rearrange("p g (t d) -> p t g d", t=2),
                                     bank[j % 4][:, :].rearrange("p (t g d) -> p t g d", t=2, g=2),
                                     ACT.Copy).then_inc(vt_in, 1)
            for j in range(4):
                act.wait_ge(vt_t, 8 + j + 1)
                nc.scalar.activation(k_tok[:, 4 * j * P:(4 * j + 4) * P], bank[j % 4][:, :], ACT.Copy).then_inc(vt_in, 1)

            def a_ckT(h):
                act.wait_ge(ck_t, h + 1)
                nc.scalar.activation(ckT[:, h % 2, :], bank[h % 2][:, 384:512], ACT.Copy).then_inc(ck_in, 1)

            def a_exp(h):
                act.wait_ge(mx_ready, h + 1)
                if h >= 2:
                    act.wait_ge(pt_t, h - 1)
                nc.scalar.activation(prob[:, h % 2, 0:128], bank[h % 2][:, 0:128], ACT.Exp,
                                     bias=smax[:, h % 2, 0:1], accum_out=ssum[:, h % 2, 0:1])
                nc.scalar.activation(prob[:, h % 2, 128:384], bank[h % 2][:, 128:384], ACT.Exp,
                                     bias=smax[:, h % 2, 1:2], accum_out=ssum[:, h % 2, 1:2]).then_inc(ex_ready, 1)

            def a_probT(h):
                act.wait_ge(pt_t, h + 1)
                nc.scalar.activation(probT[:, h % 2, :], bank[2 + h % 2][:, 0:384], ACT.Copy).then_inc(pt_in, 1)

            a_ckT(0)
            for s in range(HEADS + 2):
                if s + 1 < HEADS:
                    a_ckT(s + 1)
                if s < HEADS:
                    a_exp(s)
                if s >= 2:
                    a_probT(s - 2)

            phase(4, norm_next=True)
            act.wait_ge(kvout, 32)
            norm(G_END["wo"], ph[5])
            for k in range(5, 13):
                phase(k, norm_next=k == 12)
            norm(G_END["down0_3"], ph[13])
            phase(13)
            R = lambda j: ROOM[:, j, :]
            act.wait_ge(group_out, G_END["dt"])
            link(nc.scalar.activation(R(1), R(0), ACT.Abs))
            nc.scalar.activation(R(2), R(1), ACT.Exp, scale=-1.0).then_inc(dt_a, 1)
            nc.scalar.activation(col[:, 2:3], col[:, 1:2], ACT.Exp).then_inc(dt_a, 1)
            act.wait_ge(dt_v, 1)
            nc.scalar.activation(R(4), R(3), ACT.Ln).then_inc(dt_a, 1)
            phase(14)
            act.wait_ge(dt_t, 1)
            nc.scalar.activation(dt_tok[:, :, :], bank[4][:, 0:256].rearrange("p (r c) -> p r c", r=2), ACT.Copy)
            nc.scalar.activation(ROOM[:, 9, :], bank[4][:, 256:512], ACT.Copy).then_inc(dt_p, 1)
            act.wait_ge(dt_t, 2)
            nc.scalar.activation(ROOM[:, 10, :], bank[5][:, 0:256], ACT.Copy).then_inc(dt_p, 1)
            act.wait_ge(dt_t, 3)
            nc.scalar.activation(ac_tok[:, :, :], bank[4][:, 0:256].rearrange("p (r c) -> p r c", r=2),
                                 ACT.Copy).then_inc(dt_p, 1)
            act.wait_ge(dt_v, 4)
            nc.scalar.activation(ROOM[:, 12, 0:128], ROOM[:, 11, 0:128], ACT.Exp).then_inc(dt_a, 1)
            phase(15)

            def state_copy(g, d):
                act.wait_ge(st_pe, 2 * g + d + 1)
                if 2 * g + d:
                    act.wait_ge(st_done, 16 * (2 * g + d))
                nc.scalar.activation(s_out[:, :, :], bank[5][:, :].rearrange("p (b n) -> p b n", b=4),
                                     ACT.Copy).then_inc(st_sb, 1)

            def segments(g):
                act.wait_ge(bc_in[0][1], 16 * (g + 1))
                for e in range(8):
                    hd = SSM_HEADS + 8 * g + e
                    i = nc.scalar.activation(bc[0][:, 1, e, :], bc[0][:, 1, e, :], ACT.Relu, scale=-1.0,
                                             bias=ac_tok[:, 0, hd:hd + 1])
                i.then_inc(seg_p, 1)

            segments(0)
            for g in range(SSM_GROUPS):
                act.wait_ge(seg_v, g + 1)
                nc.scalar.activation(bc[0][:, 0, :, :], bc[0][:, 0, :, :], ACT.Exp).then_inc(dec_ready, 1)
                act.wait_ge(seg_p, g + 1)
                nc.scalar.activation(bc[0][:, 1, :, :], bc[0][:, 1, :, :], ACT.Exp, scale=-1.0).then_inc(dec_ready, 1)
                act.wait_ge(fr_t, 2 * g + 2)
                for d in range(2):
                    nc.scalar.activation(h0T[:, d, :], bank[6 + d][:, :], ACT.Copy).then_inc(h0_in, 1)
                for d in range(2):
                    act.wait_ge(bc_in[1][d], 16 * (g + 1))
                    for e in range(8):
                        hd = d * SSM_HEADS + 8 * g + e
                        i = nc.scalar.activation(bc[1][:, d, e, :], bc[1][:, d, e, :], ACT.Relu, scale=-1.0,
                                                 bias=ac_tok[:, 1, hd:hd + 1])
                    i.then_inc(seg_a, 1)
                    act.wait_ge(seg_a, 2 * g + d + 1)
                    nc.scalar.activation(bc[1][:, d, :, :], bc[1][:, d, :, :], ACT.Exp,
                                         scale=-1.0).then_inc(dec_ready, 1)
                    if d == 0:
                        state_copy(g, 0)
                act.wait_ge(ea_in, 64 * (g + 1))
                nc.scalar.activation(ea[:, :, :, :], ea[:, :, :, :], ACT.Exp).then_inc(ea_ready, 1)
                state_copy(g, 1)
                if g + 1 < SSM_GROUPS:
                    segments(g + 1)

            for t in range(8):
                act.wait_ge(yz, t + 1)
                if t >= 4:
                    act.wait_ge(ysq_pe, t - 3)
                nc.scalar.activation(ROOM[:, 32 + 4 * (t % 4):36 + 4 * (t % 4), :], ROOM[:, 4 * t:4 * t + 4, :],
                                     ACT.Square).then_inc(ysq, 1)
            split(ph[16].T0 + 1, 4, 0)
            act.wait_ge(ysq_pe, 8)
            act.wait_ge(st_done, 16 * 2 * SSM_GROUPS)
            nc.scalar.activation(rbc[:, :], STAT[:, 0:TOK], ACT.Sqrt, scale=1.0 / D_INNER,
                                 bias=col[:, 3:4]).then_inc(y_root, 1)
            for t in range(8):
                act.wait_ge(y_sc, t + 1)
                dst = (HL, HID)[t // 4]
                nc.scalar.activation(dst[:, 4 * (t % 4):4 * (t % 4) + 4, 0:TOK], ROOM[:, 4 * t:4 * t + 4, :],
                                     ACT.Copy).then_inc(y_hi, 1)
                if t < 4:
                    for c in first_splits(ph[16])[t][0] + first_splits(ph[16])[t][1]:
                        split(ph[16].T0 + c, 4, 0)
            phase(16)
            phase(17, norm_next=True)
            norm(G_END["wout1"], ph[18])
            for k in range(18, 26):
                phase(k, norm_next=k == 25)
            act.wait_ge(group_out, G_END["down1_3"])
            squares(range(3, 4))
            norm_root()
            for j in range(8):
                act.wait_ge(f_t, j + 1)
                nc.scalar.activation(y_tok[:, :, 2 * j * P:(2 * j + 2) * P].rearrange("p g (t d) -> p t g d", t=2),
                                     bank[j % 4][:, :].rearrange("p (t g d) -> p t g d", t=2, g=2),
                                     ACT.Copy).then_inc(f_sb, 1)

        @block.vector
        def _(dve):
            dsteps = [0]
            e2 = [0]

            def link(i):
                dsteps[0] += 1
                i.then_inc(dve_step, 1)
                dve.wait_ge(dve_step, dsteps[0])

            def split(T, rate, shift):
                p = owner[T]
                typ, _q = p.chunks[(T - p.T0) % p.m]
                n = HALF if typ == "M" else CH_KT // 2 * p.width
                for u in range(2):
                    dve.wait_ge(hi_ready, 2 * T + u + 1 + shift * (2 * rate))
                    s = slice(u * n, (u + 1) * n)
                    nc.vector.tensor_tensor(w_lo[:, T % 2, s], raw[:, T % RAW_SLOTS, s], w_hi[:, T % 2, s],
                                            ALU.subtract).then_inc(lo_ready, 1)

            E2_STEPS = {"w1": 2, "xbc": 2}

            def phase(k):
                p = ph[k]
                steps = E2_STEPS.get(p.kind, 0)
                e2_0 = e2[0]
                e2[0] += steps * p.n

                def finish(rep, shift):
                    gi = p.G0 + rep
                    dve.wait_ge(bank_free, 4 * (gi + 2) + 4 * shift)
                    tiles = bass.ds(4 * rep + 4 * shift, 4)
                    Uall = U[:, :, :]

                    def step(i, s):
                        i.then_inc(e2_step, 1)
                        dve.wait_ge(e2_step, e2_0 + steps * rep + s + steps * shift)
                    if p.kind in "qkv":
                        dst = {"q": qT, "k": kT, "v": vT}[p.kind]
                        i = nc.vector.tensor_scalar(dst[:, tiles, :], Uall, float(P) ** -0.5 if p.kind == "q" else 1.0,
                                                    None, ALU.mult)
                    elif p.kind == "z":
                        i = nc.vector.tensor_copy(zS[:, tiles, :], Uall)
                    elif p.kind == "dt":
                        i = nc.vector.tensor_scalar(ROOM[:, 0, :], U[:, 0, :], col[:, 0:1], None, ALU.add)
                    elif p.kind == "w1":
                        step(nc.vector.scalar_tensor_tensor(Uall, Uall, 0.0, Uall, ALU.max, ALU.mult), 1)
                        step(nc.vector.tensor_copy(HID[:, tiles, 0:TOK], Uall), 2)
                        i = nc.vector.tensor_tensor(HID[:, tiles, TOK:2 * TOK], Uall, HID[:, tiles, 0:TOK],
                                                    ALU.subtract)
                    elif p.kind == "res":
                        layer, gate = p.more["layer"], p.more["gate"]
                        for b in range(4):
                            for r in range(2):
                                xt = X[:, bass.ds(4 * rep + b + 4 * shift, 1), r * SEQ:(r + 1) * SEQ].rearrange("p o t -> p (o t)")
                                gt = modv[:, layer, bass.ds(gate + 4 * rep + b + 4 * shift, 1), r]
                                i = nc.vector.scalar_tensor_tensor(xt, U[:, b, r * SEQ:(r + 1) * SEQ], gt, xt,
                                                                   ALU.mult, ALU.add)
                    elif p.kind == "xbc":
                        def par(s, r0, b):
                            return PAR[:, s, bass.ds(r0 + 4 * rep + b + 4 * shift, 1)]
                        for b in range(4):
                            o = ROOM[:, bass.ds(4 * rep + b + 4 * shift, 1), :].rearrange("p o t -> p (o t)")
                            i = nc.vector.tensor_scalar(o, U[:, b, :], par(2, 48, b), par(3, 48, b), ALU.mult, ALU.add)
                        step(i, 1)
                        for b in range(4):
                            o = ROOM[:, bass.ds(4 * rep + b + 4 * shift, 1), :].rearrange("p o (r t) -> p (o r) t", r=2)
                            u = U[:, b, :].rearrange("p (r t) -> p r t", r=2)
                            i = nc.vector.scalar_tensor_tensor(o[:, :, 1:SEQ], u[:, :, 0:SEQ - 1], par(2, 0, b),
                                                               o[:, :, 1:SEQ], ALU.mult, ALU.add)
                        step(i, 2)
                        for b in range(4):
                            o = ROOM[:, bass.ds(4 * rep + b + 4 * shift, 1), :].rearrange("p o (r t) -> p (o r) t", r=2)
                            u = U[:, b, :].rearrange("p (r t) -> p r t", r=2)
                            i = nc.vector.scalar_tensor_tensor(o[:, :, 0:SEQ - 1], u[:, :, 1:SEQ], par(3, 0, b),
                                                               o[:, :, 0:SEQ - 1], ALU.mult, ALU.add)
                    i.then_inc(group_out, 1)

                def mod_bias(rep, shift):
                    mg = p.M0 + rep
                    layer, g0 = p.mod
                    dve.wait_ge(m_cols, mg + 1 + shift)
                    first = 4 * (g0 + rep)
                    bias = PAR[:, layer, bass.ds(first + 4 * shift, 4)].unsqueeze(2).to_broadcast([P, 4, 2])
                    nc.vector.tensor_tensor(modv[:, layer, bass.ds(first + 4 * shift, 4), :],
                                            MCOL[:, 0:8].rearrange("p (b v) -> p b v", b=4), bias,
                                            ALU.add).then_inc(mod_out, 1)

                def body(rep, shift):
                    early = 3 if p.pat == "LM" else 2
                    for c in range(1, p.m):
                        if c == early and rep and "L" in p.pat:
                            finish(rep - 1, shift)
                        if c == early and rep and "M" in p.pat:
                            mod_bias(rep - 1, shift)
                        if rep or k not in after_norm:
                            split(p.T0 + rep * p.m + c, p.m, shift)
                    nxt = p.T0 + (rep + 1) * p.m
                    if nxt < N_CHUNKS:
                        split(nxt, p.m, shift)
                    if "L" in p.pat:
                        gi = p.G0 + rep
                        for b in range(p.width // P):
                            dve.wait_ge(evac, 4 * gi + (b + 1 if p.width == CH_N else 4) + 4 * shift)
                            i = nc.vector.tensor_tensor(U[:, b, :], bank[b][:, 0:TOK], U[:, b, :], ALU.add)
                            i.then_inc(bank_free, 1 if p.width == CH_N else 4)
                    if rep == p.n - 1:
                        if "L" in p.pat:
                            finish(rep, 0)
                        if "M" in p.pat:
                            mod_bias(rep, 0)
                runs(dve, p, body)

            norms = [0]

            def norm(layer, scale, shift_, gain, p=None, last=False):
                k = norms[0]
                norms[0] += 1
                if not last:
                    dve.wait_ge(mod_out, 1 + max(p.M0 + p.n for p in ph if "M" in p.pat and p.T0 < cur[0]))
                    g = gain.unsqueeze(2).to_broadcast([P, KT, 2])
                    link(nc.vector.scalar_tensor_tensor(modA[:, :, :], modv[:, layer, scale:scale + KT, :], 1.0, g,
                                                        ALU.add, ALU.mult))
                    split(p.T0 + 1, p.m, 0)
                dve.wait_ge(rms_root, k + 1)
                link(nc.vector.reciprocal(rbc[:, :], rbc[:, :]))
                r4 = rbc[:, :].unsqueeze(1).to_broadcast([P, 4, TOK])

                def lo(t):
                    dve.wait_ge(oper_hi, 4 * k + t + 1)
                    s = slice(4 * t, 4 * t + 4)
                    nc.vector.tensor_tensor(HL[:, s, TOK:2 * TOK], SQ[:, s, :], HL[:, s, 0:TOK],
                                            ALU.subtract).then_inc(oper, 1)
                for t in range(4):
                    s = slice(4 * t, 4 * t + 4)
                    if last:
                        link(nc.vector.tensor_tensor(SQ[:, s, :], X[:, s, :], r4, ALU.mult))
                        g4 = gain[:, s].unsqueeze(2).to_broadcast([P, 4, TOK])
                        nc.vector.tensor_tensor(SQ[:, s, :], SQ[:, s, :], g4, ALU.mult).then_inc(f_sc, 1)
                        continue
                    v = SQ[:, s, :].rearrange("p t (r c) -> p (t r) c", r=2)
                    for j in range(4 * t, 4 * t + 4):
                        for r in range(2):
                            c = slice(r * SEQ, (r + 1) * SEQ)
                            i = nc.vector.scalar_tensor_tensor(SQ[:, j, c], X[:, j, c], modA[:, j, r:r + 1],
                                                               rbc[:, c], ALU.mult, ALU.mult)
                    link(i)
                    b = modv[:, layer, shift_ + 4 * t:shift_ + 4 * t + 4, :].rearrange("p t r -> p (t r)") \
                        .unsqueeze(2).to_broadcast([P, 8, SEQ])
                    nc.vector.tensor_tensor(v, v, b, ALU.add).then_inc(scaled, 1)
                    before, after = first_splits(p)[t]
                    for c in before:
                        split(p.T0 + c, p.m, 0)
                    lo(t)
                    for c in after:
                        split(p.T0 + c, p.m, 0)

            cur = [0]

            dve.sem_inc(bank_free, 4)
            dve.sem_inc(mod_out, 1)
            nc.vector.memset(col[:, 3:4], NORM_EPS)
            nc.vector.memset(cond_w[:, KT * 4:].bitcast(F32), 0.0)
            nc.vector.memset(one[:, :], 1.0).then_inc(init, 1)
            dve.wait_ge(par_t, 1)
            nc.vector.tensor_copy(PAR[:, 0:4, :], bank[0][:, :].rearrange("p (s c) -> p s c", s=4)).then_inc(par_in, 1)
            dve.wait_ge(par_t, 2)
            nc.vector.tensor_copy(PAR[:, 4, 0:16], bank[1][:, 0:16]).then_inc(par_in, 1)
            dve.wait_ge(cond_in, 2)
            nc.vector.tensor_tensor(cond[:, :, 2:4], csil[:, :, :].rearrange("p v t -> p t v"), cond[:, :, 0:2],
                                    ALU.subtract).then_inc(cond_in, 1)
            split(0, 4, 0)
            for j in range(8):
                dve.wait_ge(x_t, j + 1)
                nc.vector.tensor_copy(X[:, 2 * j:2 * j + 2, :],
                                      bank[2 + j % 4][:, :].rearrange("p (t c) -> p t c", t=2)).then_inc(x_in, 1)
            dve.wait_ge(gin, 96)
            for h in range(2):
                q = slice(64 * h, 64 * h + 64)
                nc.vector.tensor_tensor(d_sum[q, :], d_all[q, 0, h::2], d_all[q, 1, h::2], ALU.add)
            dve.wait_ge(bin_, 64)
            keep = win[:, 0:1, :].to_broadcast([P, HEADS, P])
            neg = win[:, 1:2, :].to_broadcast([P, HEADS, P])
            link(nc.vector.tensor_tensor(biasm[:, :, :], biasm[:, :, :], keep, ALU.mult))
            link(nc.vector.tensor_tensor(biasm[:, :, :], biasm[:, :, :], neg, ALU.add))
            phase(0)
            dve.wait_ge(x_in, 8)
            cur[0] = ph[1].T0
            norm(0, KT, 0, PAR[:, 1, 96:112], ph[1])
            phase(1)
            phase(2)
            phase(3)

            def d_max(h):
                dve.wait_ge(sc_ready, h + 1)
                nc.vector.reduce_max(smax[:, h % 2, 0:1], bank[h % 2][:, 0:128], AX.X, negate=True)
                nc.vector.reduce_max(smax[:, h % 2, 1:2], bank[h % 2][:, 128:384], AX.X,
                                     negate=True).then_inc(mx_ready, 1)

            def d_norm(h):
                dve.wait_ge(ex_ready, h + 1)
                link(nc.vector.reciprocal(ssum[:, h % 2, :], ssum[:, h % 2, :]))
                nc.vector.tensor_scalar(prob[:, h % 2, 0:128], prob[:, h % 2, 0:128], ssum[:, h % 2, 0:1], None, ALU.mult)
                nc.vector.tensor_scalar(prob[:, h % 2, 128:384], prob[:, h % 2, 128:384], ssum[:, h % 2, 1:2], None,
                                        ALU.mult).then_inc(pr_ready, 1)

            def d_out(h):
                dve.wait_ge(o_ready, h + 1)
                link(nc.vector.tensor_copy(HID[:, h, 0:TOK], bank[4 + h % 2][:, 0:TOK]))
                nc.vector.tensor_tensor(HID[:, h, TOK:2 * TOK], bank[4 + h % 2][:, 0:TOK], HID[:, h, 0:TOK],
                                        ALU.subtract).then_inc(oper, 1)

            for s in range(HEADS + 3):
                if s < HEADS:
                    d_max(s)
                if 1 <= s <= HEADS:
                    d_norm(s - 1)
                if s >= 3:
                    d_out(s - 3)

            phase(4)
            dve.wait_ge(kvout, 32)
            cur[0] = ph[5].T0
            norm(0, 4 * KT, 3 * KT, PAR[:, 2, 96:112], ph[5])
            for k in range(5, 13):
                phase(k)
            cur[0] = ph[13].T0
            norm(1, KT, 0, PAR[:, 1, 112:128], ph[13])
            phase(13)
            R = lambda j: ROOM[:, j, :]
            dve.wait_ge(dt_a, 1)
            nc.vector.tensor_scalar(R(3), R(2), 1.0, None, ALU.add).then_inc(dt_v, 1)
            dve.wait_ge(dt_v, 1)
            link(nc.vector.tensor_scalar(R(5), R(3), 1.0, None, ALU.subtract))
            link(nc.vector.tensor_tensor(R(5), R(5), R(2), ALU.subtract))
            link(nc.vector.reciprocal(R(6), R(3)))
            link(nc.vector.tensor_tensor(R(5), R(5), R(6), ALU.mult))
            dve.wait_ge(dt_a, 3)
            link(nc.vector.tensor_tensor(R(4), R(4), R(5), ALU.subtract))
            link(nc.vector.scalar_tensor_tensor(R(7), R(0), 0.0, R(4), ALU.max, ALU.add))
            nc.vector.tensor_scalar(R(8), R(7), col[:, 2:3], -1.0, ALU.mult, ALU.mult).then_inc(dt_v, 1)
            phase(14)
            dve.wait_ge(dt_t, 4)
            dve.wait_ge(dt_p, 3)
            dve.wait_ge(group_out, G_END["z"])
            nc.vector.tensor_tensor(ROOM[:, 11, 0:128], bank[5][:, 256:384], ac_tok[:, 0, :], ALU.subtract).then_inc(dt_v, 1)
            dve.sem_inc(dt_v, 1)
            dve.wait_ge(dt_a, 4)
            link(nc.vector.tensor_tensor(w_end[:, :], ROOM[:, 12, 0:128], dt_tok[:, 0, :], ALU.mult))
            dve.wait_ge(ac_w, 16)
            phase(15)

            def segments(g):
                dve.wait_ge(bc_in[0][0], 16 * (g + 1))
                for e in range(8):
                    hd = 8 * g + e
                    i = nc.vector.tensor_scalar(bc[0][:, 0, e, :], bc[0][:, 0, e, :], ac_tok[:, 0, hd:hd + 1],
                                                0.0, ALU.subtract, ALU.min)
                i.then_inc(seg_v, 1)

            def weighted_x(g, kind):
                r = kind % 2
                for d in range(2):
                    hd = d * SSM_HEADS + 8 * g
                    w = (w_end[:, hd:hd + 8] if kind == 2 else dt_tok[:, r, hd:hd + 8]).unsqueeze(2).to_broadcast([P, 8, 64])
                    i = nc.vector.tensor_tensor(xd[:, kind, d, :].rearrange("p (h c) -> p h c", h=8),
                                                bank[r][:, :].rearrange("p (h c) -> p h c", h=8), w, ALU.mult)
                return i

            def y_base(g, r):
                dve.wait_ge(unit_pe, 4 * g + 2 * r + 2)
                for j in range(4):
                    xt = ROOM[:, 4 * g + j, r * SEQ:(r + 1) * SEQ]
                    i = nc.vector.scalar_tensor_tensor(xt, xt, d_sum[:, 4 * g + j:4 * g + j + 1],
                                                       bank[3 + r][:, j * P:(j + 1) * P], ALU.mult, ALU.add)
                return i

            def front(g):
                dve.wait_ge(fx_t, g + 1)
                if g:
                    dve.wait_ge(mm_ready, 4 * g)
                for r in range(2):
                    for d in range(2):
                        i = nc.vector.tensor_tensor(cbm[:, r, d, :], bank[2][:, r * P:(r + 1) * P], tri[:, d, :], ALU.mult)
                i.then_inc(cb_ready, 1)
                if g:
                    dve.wait_ge(st_pe, 2 * g)
                nc.vector.tensor_copy(b_tok[:, 0:128], bank[2][:, 256:384]).then_inc(bt_in, 1)
                if g:
                    dve.wait_ge(unit_pe, 4 * g - 2)
                weighted_x(g, 2)
                weighted_x(g, 0).then_inc(xd_ready, 1)

            def decayed(g, r, d):
                dve.wait_ge(dec_ready, 4 * g + 2 * r + d + 1)
                m = cbm[:, r, d:d + 1, :].to_broadcast([P, 8, P])
                nc.vector.tensor_tensor(bc[r][:, d, :, :], bc[r][:, d, :, :], m, ALU.mult).then_inc(mm_ready, 1)

            def y_sample(g):
                dve.wait_ge(ea_used, g + 1)
                link(y_base(g, 1))
                xa = ROOM[:, 4 * g:4 * g + 4, SEQ:]
                link(nc.vector.tensor_tensor(xa, xa, ea[:, 0, :, :], ALU.add))
                nc.vector.tensor_tensor(xa, xa, ea[:, 1, :, :], ALU.add).then_inc(y_sb, 1)

            segments(0)
            front(0)
            for g in range(SSM_GROUPS):
                dve.wait_ge(cb_ready, g + 1)
                decayed(g, 0, 0)
                decayed(g, 0, 1)
                if g:
                    y_sample(g - 1)
                weighted_x(g, 1).then_inc(xd_ready, 1)
                decayed(g, 1, 0)
                y_base(g, 0).then_inc(y_sb, 1)
                decayed(g, 1, 1)
                if g + 1 < SSM_GROUPS:
                    segments(g + 1)
                dve.wait_ge(ea_ready, g + 1)
                for d in range(2):
                    dve.wait_ge(yo_pe, 2 * g + d + 1)
                    i = nc.vector.tensor_tensor(ea[:, d, :, :], ea[:, d, :, :],
                                                bank[6 + d][:, :].rearrange("p (b l) -> p b l", b=4), ALU.mult)
                i.then_inc(ea_used, 1)
                if g + 1 < SSM_GROUPS:
                    front(g + 1)
            y_sample(SSM_GROUPS - 1)

            for t in range(8):
                dve.wait_ge(silu_out, 20)
                dve.wait_ge(y_sb, 16)
                s = slice(4 * t, 4 * t + 4)
                nc.vector.tensor_tensor(ROOM[:, s, :], ROOM[:, s, :], zS[:, s, :], ALU.mult).then_inc(yz, 1)
            dve.wait_ge(yz, 8)
            split(ph[16].T0 + 1, 4, 0)
            dve.wait_ge(y_root, 1)
            dve.wait_ge(st_done, 16 * 2 * SSM_GROUPS)
            link(nc.vector.reciprocal(rbc[:, :], rbc[:, :]))
            r4 = rbc[:, :].unsqueeze(1).to_broadcast([P, 4, TOK])

            def y_lo(t):
                dve.wait_ge(y_hi, t + 1)
                dst = (HL, HID)[t // 4]
                s = slice(4 * (t % 4), 4 * (t % 4) + 4)
                nc.vector.tensor_tensor(dst[:, s, TOK:2 * TOK], ROOM[:, 4 * t:4 * t + 4, :], dst[:, s, 0:TOK],
                                        ALU.subtract).then_inc(y_op, 1)
            for t in range(8):
                s = slice(4 * t, 4 * t + 4)
                link(nc.vector.tensor_tensor(ROOM[:, s, :], ROOM[:, s, :], r4, ALU.mult))
                g4 = PAR[:, 3, 96 + 4 * t:100 + 4 * t].unsqueeze(2).to_broadcast([P, 4, TOK])
                nc.vector.tensor_tensor(ROOM[:, s, :], ROOM[:, s, :], g4, ALU.mult).then_inc(y_sc, 1)
                if t < 4:
                    before, after = first_splits(ph[16])[t]
                    for c in before:
                        split(ph[16].T0 + c, 4, 0)
                    y_lo(t)
                    for c in after:
                        split(ph[16].T0 + c, 4, 0)
                elif t > 4:
                    y_lo(t - 1)
            y_lo(7)
            phase(16)
            phase(17)
            cur[0] = ph[18].T0
            norm(1, 4 * KT, 3 * KT, PAR[:, 2, 112:128], ph[18])
            for k in range(18, 26):
                phase(k)
            norm(1, 0, 0, PAR[:, 4, 0:16], last=True)

        @block.tensor
        def _(pe):
            def phase(k, ready):
                p = ph[k]
                A = {"HL": HL, "HID": HID, None: None}[p.operand]
                nb = p.width // P

                def body(s):
                    for c, (typ, q) in enumerate(p.chunks):
                        T = p.T0 + c
                        slot = T % 2
                        if typ == "M":
                            for u in range(2):
                                pe.wait_ge(lo_ready, 2 * T + u + 1 + s * (2 * p.m))
                                for kk in range(2):
                                    kt = 2 * u + kk
                                    at = 4 * (4 * q + kt)
                                    lhs = cond_w[:, at:at + P]
                                    for part, w in enumerate((w_hi, w_lo)):
                                        first = q == 0 and kt == 0 and part == 0
                                        last = q == 3 and kt == 3 and part == 1
                                        i = nc.tensor.matmul(MROW[:, :], lhs, w[:, slot, kt * CH_N:(kt + 1) * CH_N],
                                                             start=first, stop=last)
                                i.then_inc(w_read, 2)
                            continue
                        n = p.width
                        sem_, value = ready(q)
                        pe.wait_ge(sem_, value)
                        block_order = by_block(p, c)

                        def products(b, kts):
                            for kt in kts:
                                hi = w_hi[:, slot, kt * n + b * P:kt * n + (b + 1) * P]
                                lo = w_lo[:, slot, kt * n + b * P:kt * n + (b + 1) * P]
                                first, last = q == 0 and kt == 0, q == 3 and kt == 3
                                a = A[:, 4 * q + kt, :]
                                if not first:
                                    nc.tensor.matmul(bank[b][:, 0:TOK], lo, a[:, 0:TOK], start=False, stop=False)
                                i = nc.tensor.matmul(bank[b][:, :], hi, a, start=first, stop=last)
                                if first:
                                    i = nc.tensor.matmul(bank[b][:, 0:TOK], lo, a[:, 0:TOK], start=False, stop=False)
                            return i

                        def bank_wait(b):
                            if q == 0:
                                pe.wait_ge(bank_free, 4 * p.G0 + b + 1 + s * 4)
                        if block_order:
                            for b in range(nb):
                                bank_wait(b)
                                if b == 0:
                                    pe.wait_ge(lo_ready, 2 * T + 1 + s * (2 * p.m))
                                    products(b, (0, 1))
                                    pe.wait_ge(lo_ready, 2 * T + 2 + s * (2 * p.m))
                                products(b, (2, 3) if b == 0 else range(4)).then_inc(w_read, 4 // nb)
                        else:
                            for u in range(2):
                                pe.wait_ge(lo_ready, 2 * T + u + 1 + s * (2 * p.m))
                                for b in range(nb):
                                    if u == 0:
                                        bank_wait(b)
                                    i = products(b, (2 * u, 2 * u + 1))
                                i.then_inc(w_read, 2)
                    if "M" in p.pat:
                        pe.wait_ge(m_rows_in, p.M0 + 1 + s)
                        pe.wait_ge(mod_out, p.M0 + 1 + s)
                        for b in range(4):
                            i = nc.tensor.matmul(MCOL[:, 2 * b:2 * b + 2], m_rows[:, b * P:(b + 1) * P], comb[:, :],
                                                 start=True, stop=True)
                        i.then_inc(m_cols, 1)
                if p.n == 1:
                    body(0)
                else:
                    with pe.Fori(0, p.n) as s:
                        body(s)

            norms = [0]
            ones = one[:, 0:1].to_broadcast([P, P])

            def norm():
                for k in range(KT):
                    if k % 4 == 0:
                        pe.wait_ge(sq_ready, 4 * norms[0] + k // 4 + 1)
                    i = nc.tensor.matmul(STAT[:, 0:TOK], ones, SQ[:, k, :], start=k == 0, stop=k == KT - 1)
                i.then_inc(stat_ready, 1)
                norms[0] += 1

            pe.wait_ge(cin, 32)
            pe.wait_ge(rin, 16 * 14)
            for s in range(4):
                i = nc.tensor.transpose(bank[0][:, s * P:(s + 1) * P], rows[:, s, :], ident[:, :])
            i.then_inc(par_t, 1)
            nc.tensor.transpose(bank[1][:, 0:16], rows[0:16, 4, :], ident[0:16, 0:16]).then_inc(par_t, 1)
            pe.wait_ge(xin, 32)
            pe.wait_ge(init, 1)
            for j in range(8):
                if j >= 4:
                    pe.wait_ge(x_in, j - 3)
                for t in range(2):
                    for r in range(2):
                        f = (2 * j + t) * P
                        i = nc.tensor.transpose(bank[2 + j % 4][:, (2 * t + r) * P:(2 * t + r + 1) * P],
                                                x_tok[:, r, f:f + P], ident[:, :])
                i.then_inc(x_t, 1)
            pe.wait_ge(cond_in, 3)
            phase(0, None)
            norm()
            pe.wait_ge(rms_root, 1)
            for k in (1, 2, 3):
                phase(k, lambda q: (oper, q + 1))

            pe.wait_ge(group_out, G_END["v"])
            for j in range(8):
                if j < 4:
                    pe.wait_ge(bank_free, 4 * G_END["v"] + 4)
                else:
                    pe.wait_ge(vt_in, j - 3)
                for t in range(2):
                    for r in range(2):
                        i = nc.tensor.transpose(bank[j % 4][:, (2 * t + r) * P:(2 * t + r + 1) * P],
                                                vT[:, 2 * j + t, r * SEQ:(r + 1) * SEQ], ident[:, :])
                i.then_inc(vt_t, 1)
            for j in range(4):
                pe.wait_ge(vt_in, 5 + j)
                for t in range(4):
                    i = nc.tensor.transpose(bank[j % 4][:, t * P:(t + 1) * P], kT[:, 4 * j + t, 0:SEQ], ident[:, :])
                i.then_inc(vt_t, 1)
            pe.wait_ge(vt_in, 12)
            pe.wait_ge(kv_in, 32)

            def p_ckT(h):
                if h >= 2:
                    pe.wait_ge(ex_ready, h - 1)
                nc.tensor.transpose(bank[h % 2][:, 384:512], ck[:, h * P:(h + 1) * P], ident[:, :]).then_inc(ck_t, 1)

            def p_scores(h):
                pe.wait_ge(ck_in, h + 1)
                S = bank[h % 2]
                nc.tensor.matmul(S[:, 0:128], qT[:, h, 0:SEQ], kT[:, h, 0:SEQ], start=True, stop=True)
                nc.tensor.matmul(S[:, 128:256], flip[:, :], biasm[:, h, :], start=True, stop=False)
                nc.tensor.matmul(S[:, 128:256], qT[:, h, SEQ:], kT[:, h, SEQ:], start=False, stop=True)
                nc.tensor.matmul(S[:, 256:384], qT[:, h, SEQ:], ckT[:, h % 2, :], start=True, stop=True).then_inc(sc_ready, 1)

            def p_probT(h):
                pe.wait_ge(pr_ready, h + 1)
                if h >= 2:
                    pe.wait_ge(pt_in, h - 1)
                for j in range(3):
                    i = nc.tensor.transpose(bank[2 + h % 2][:, j * P:(j + 1) * P], prob[:, h % 2, j * P:(j + 1) * P], ident[:, :])
                i.then_inc(pt_t, 1)

            def p_out(h):
                pe.wait_ge(pt_in, h + 1)
                if h >= 2:
                    pe.wait_ge(oper, 4 + h - 1)
                O = bank[4 + h % 2]
                hs = slice(h * P, (h + 1) * P)
                nc.tensor.matmul(O[:, 0:128], v_tok[:, 0, hs], probT[:, h % 2, 0:128], start=True, stop=True)
                nc.tensor.matmul(O[:, 128:256], v_tok[:, 1, hs], probT[:, h % 2, 128:256], start=True, stop=False)
                nc.tensor.matmul(O[:, 128:256], cv[:, hs], probT[:, h % 2, 256:384], start=False, stop=True).then_inc(o_ready, 1)

            p_ckT(0)
            for s in range(HEADS + 3):
                if s < HEADS:
                    p_scores(s)
                if 2 <= s < HEADS + 2:
                    p_probT(s - 2)
                if s >= 3:
                    p_out(s - 3)
                if s + 1 < HEADS:
                    p_ckT(s + 1)

            phase(4, lambda q: (oper, 4 + 4 * (q + 1)))
            norm()
            base_op = [20]

            def mlp(k0):
                for q_ in range(N_QUARTERS):
                    phase(k0 + 2 * q_, lambda q, b=base_op[0]: (oper, b + q + 1))
                    phase(k0 + 2 * q_ + 1, lambda q, g=ph[k0 + 2 * q_].G0: (group_out, g + q + 1))
            mlp(5)
            norm()
            phase(13, lambda q: (oper, 24 + q + 1))
            phase(14, lambda q: (oper, 24 + q + 1))
            pe.wait_ge(dt_v, 2)
            pe.wait_ge(gin, 96)
            for n in range(2):
                for r in range(2):
                    i = nc.tensor.transpose(bank[4][:, (2 * n + r) * P:(2 * n + r + 1) * P],
                                            ROOM[:, 7 + n, r * SEQ:(r + 1) * SEQ], ident[:, :])
            i.then_inc(dt_t, 1)
            pe.wait_ge(dt_p, 1)
            for r in range(2):
                for d in range(2):
                    i = nc.tensor.matmul(bank[5][64 * d:64 * d + 64, r * SEQ:(r + 1) * SEQ],
                                         ROOM[:, 9, r * P + 64 * d:r * P + 64 * d + 64], tri[:, d, :], start=True, stop=True)
            i.then_inc(dt_t, 1)
            pe.wait_ge(dt_p, 2)
            for r in range(2):
                i = nc.tensor.transpose(bank[4][:, r * P:(r + 1) * P], ROOM[:, 10, r * SEQ:(r + 1) * SEQ], ident[:, :])
            i.then_inc(dt_t, 1)
            nc.tensor.matmul(bank[5][:, 256:384], ones, ROOM[:, 9, 0:P], start=True, stop=True).then_inc(dt_t, 1)
            phase(15, lambda q: (oper, 24 + q + 1))

            pe.wait_ge(bank_free, 4 * G_END["xbc"] + 4)
            pe.wait_ge(silu_out, 20)
            def views(g):
                return ROOM[:, XT_TILES + g, :], ROOM[:, XT_TILES + SSM_GROUPS + g, :]

            def front_x(g):
                Bt, Ct = views(g)
                if g:
                    pe.wait_ge(xd_ready, 2 * g)
                for r in range(2):
                    for j in range(4):
                        nc.tensor.transpose(bank[r][:, j * P:(j + 1) * P], ROOM[:, 4 * g + j, r * SEQ:(r + 1) * SEQ], ident[:, :])
                    nc.tensor.matmul(bank[2][:, r * P:(r + 1) * P], Bt[:, r * SEQ:(r + 1) * SEQ],
                                     Ct[:, r * SEQ:(r + 1) * SEQ], start=True, stop=True)
                nc.tensor.transpose(bank[2][:, 256:384], Bt[:, 0:SEQ], ident[:, :]).then_inc(fx_t, 1)

            def front_h(g):
                if g:
                    pe.wait_ge(ea_used, g)
                pe.wait_ge(si_in, 32 * (g + 1))
                for d in range(2):
                    for j in range(4):
                        i = nc.tensor.transpose(bank[6 + d][:, j * P:(j + 1) * P], s_in[:, j, d * P:(d + 1) * P], ident[:, :])
                    i.then_inc(fr_t, 1)

            def unit(g, r, d):
                pe.wait_ge(mm_ready, 4 * g + 2 * r + d + 1)
                if g and d == 0:
                    pe.wait_ge(y_sb, 2 * g - 1 + r)
                for e in range(8):
                    o = 64 * (e % 2)
                    i = nc.tensor.matmul(bank[3 + r][o:o + 64, (e // 2) * P:(e // 2 + 1) * P],
                                         xd[:, r, d, 64 * e:64 * e + 64], bc[r][:, d, e, :],
                                         start=d == 0 and e < 2, stop=d == 1, skip_group_check=True)
                i.then_inc(unit_pe, 1)

            def end_state(g, d):
                if 2 * g + d:
                    pe.wait_ge(st_sb, 2 * g + d)
                for j in range(4):
                    i = nc.tensor.matmul(bank[5][:, j * P:(j + 1) * P], xd[:, 2, d, j * P:(j + 1) * P],
                                         b_tok[:, 0:P], start=True, stop=True)
                i.then_inc(st_pe, 1)

            front_x(0)
            front_h(0)
            for g in range(SSM_GROUPS):
                pe.wait_ge(bt_in, g + 1)
                pe.wait_ge(xd_ready, 2 * g + 1)
                end_state(g, 0)
                unit(g, 0, 0)
                unit(g, 0, 1)
                if g + 1 < SSM_GROUPS:
                    front_x(g + 1)
                end_state(g, 1)
                pe.wait_ge(h0_in, 2 * g + 2)
                _, Ct = views(g)
                for d in range(2):
                    for j in range(4):
                        i = nc.tensor.matmul(bank[6 + d][:, j * P:(j + 1) * P], h0T[:, d, j * P:(j + 1) * P],
                                             Ct[:, SEQ:], start=True, stop=True)
                    i.then_inc(yo_pe, 1)
                pe.wait_ge(xd_ready, 2 * g + 2)
                unit(g, 1, 0)
                unit(g, 1, 1)
                if g + 1 < SSM_GROUPS:
                    front_h(g + 1)

            for t in range(8):
                pe.wait_ge(ysq, t + 1)
                for j in range(4):
                    i = nc.tensor.matmul(STAT[:, 0:TOK], ones, ROOM[:, 32 + 4 * (t % 4) + j, :],
                                         start=t == 0 and j == 0, stop=t == 7 and j == 3)
                i.then_inc(ysq_pe, 1)
            phase(16, lambda q: (y_op, q + 1))
            phase(17, lambda q: (y_op, 4 + q + 1))
            norm()
            base_op[0] = 28
            mlp(18)
            norm()
            for j in range(8):
                pe.wait_ge(f_sc, j // 2 + 1)
                if j < 4:
                    pe.wait_ge(bank_free, 4 * G_END["down1_3"] + 4)
                else:
                    pe.wait_ge(f_sb, j - 3)
                for t in range(2):
                    for r in range(2):
                        i = nc.tensor.transpose(bank[j % 4][:, (2 * t + r) * P:(2 * t + r + 1) * P],
                                                SQ[:, 2 * j + t, r * SEQ:(r + 1) * SEQ], ident[:, :])
                i.then_inc(f_t, 1)


_INS = ["x_prompt", "x_sample", "cache_attn_k", "cache_attn_v", "state_ssm", "c", "c_ctx", "mod_w", "mod_b",
        "norm_mix", "norm_mlp", "mlp_w1", "mlp_w2", "na_wqkv", "na_wo", "na_rpb", "ssm_w_in", "ssm_conv_w",
        "ssm_conv_b", "ssm_dt_bias", "ssm_a_log", "ssm_d", "ssm_norm", "ssm_w_out", "final_norm"]
_OUTS = [("y_prompt", (1, 128, 2048)), ("y_sample", (1, 128, 2048)), ("new_k", (1, 1, 128, 16, 128)),
         ("new_v", (1, 1, 128, 16, 128)), ("new_state", (1, 1, 2, 64, 64, 128))]


def constants():
    c = np.zeros((P, 7, P), np.float32)
    t = np.arange(P)
    c[:, 0] = np.eye(P)
    c[:, 1] = t[:, None] <= t[None, :]
    c[:, 2] = t[:, None] >= t[None, :]
    qc, kc = t[:, None] % GRID_W, t[None, :] % GRID_W
    start = np.clip(qc - WIN_COLS // 2, 0, GRID_W - WIN_COLS)
    ok = (kc >= start) & (kc < start + WIN_COLS)
    c[:, 6] = (t[:, None] // GRID_W == t[None, :] // GRID_W) & (qc == GRID_W - 1 - kc)
    turned = np.argmax(c[:, 6], 1)
    c[:, 3] = ok[turned]
    c[:, 4] = np.where(ok[turned], 0.0, NEG)
    c[[0, 1, 2, 3], 5, [0, 1, 0, 1]] = 1.0
    return c


def kernel(**inputs):
    import numpy as _np
    import concourse.bacc as _bacc
    from concourse import mybir as _mybir
    from concourse.bass_utils import run_bass_kernel_spmd as _run

    nc = _bacc.Bacc("TRN2", target_bir_lowering=False, num_devices=1, dynamic_dma_scratch_size=8192)
    arrays = {f"in_{name}": _np.ascontiguousarray(inputs[name]) for name in _INS}
    arrays["in_consts"] = constants()
    ins = {name[3:]: nc.dram_tensor(name, a.shape, _mybir.dt.from_np(a.dtype), kind="ExternalInput").ap()
           for name, a in arrays.items()}
    outs = {name: nc.dram_tensor(f"out_{name}", shape, _mybir.dt.float32, kind="ExternalOutput").ap()
            for name, shape in _OUTS}
    program(nc, ins, outs)
    r = _run(nc, [arrays], core_ids=[0])
    return tuple(r.results[0][f"out_{name}"] for name, _ in _OUTS)
```
